# Optimizing a Trainium2 kernel written in Bass

```python
import math
import jax, jax.numpy as jnp
from jax import lax
import numpy as np

D_MODEL = 1024
BATCH = 1
SEQ = 2048
DEPTH = 1

CHUNK = 64
D_MIX = D_MODEL
D_ATTN = D_MIX // 2
D_LRU = D_MIX - D_ATTN
N_ATTN_HEADS = 8
HEAD_DIM = D_ATTN // N_ATTN_HEADS
N_LRU_BLOCKS = 8
LRU_BLOCK = D_LRU // N_LRU_BLOCKS
LRU_CONV_W = 4
LRU_C = 8.0
LEFT_CHUNKS = 8
BAND = (LEFT_CHUNKS + 1) * CHUNK
MAX_REL = 128
N_REL = (CHUNK - 1) + MAX_REL + 1
D_FF = 2816
FFN_CONV_W = 3
D_IN = 3 * D_ATTN + 2 * D_LRU
ALPHA = (2 * DEPTH) ** 0.25
BETA = (8 * DEPTH) ** -0.25
LN_EPS = 1e-5
NEG_INF = -1e30

kernel_name = "hymba_rglru_chunkattn_convffn_deepnorm"

def layer_norm(x, g, b):
    xf = x.astype(jnp.float32)
    mu = jnp.mean(xf, axis=-1, keepdims=True)
    var = jnp.mean(jnp.square(xf - mu), axis=-1, keepdims=True)
    y = (xf - mu) * lax.rsqrt(var + LN_EPS)
    return (y * g.astype(jnp.float32) + b.astype(jnp.float32)).astype(x.dtype)

def causal_dwconv(x, w, b):
    k_w = w.shape[0]
    s = x.shape[1]
    xp = jnp.pad(x, ((0, 0), (k_w - 1, 0), (0, 0)))
    y = b
    for k in range(k_w):
        y = y + w[k] * xp[:, k:k + s]
    return y

def rg_lru(x, w_a, b_a, w_x, b_x, lam):
    bsz, s, _ = x.shape
    xb = x.reshape(bsz, s, N_LRU_BLOCKS, LRU_BLOCK)
    r = jax.nn.sigmoid(jnp.einsum('bshi,hij->bshj', xb, w_a).reshape(bsz, s, D_LRU) + b_a)
    i = jax.nn.sigmoid(jnp.einsum('bshi,hij->bshj', xb, w_x).reshape(bsz, s, D_LRU) + b_x)
    log_a = -LRU_C * r.astype(jnp.float32) * jax.nn.softplus(-lam.astype(jnp.float32))
    a = jnp.exp(log_a)
    mult = jnp.sqrt(-jnp.expm1(2.0 * log_a))
    u = mult * (i * x).astype(jnp.float32)

    def combine(left, right):
        a1, b1 = left
        a2, b2 = right
        return a1 * a2, a2 * b1 + b2

    _, h = lax.associative_scan(combine, (a, u), axis=1)
    return h.astype(x.dtype)

def chunk_band_attention(q, k, v, rel_table):
    bsz, s, _ = q.shape
    nc = s // CHUNK
    shp = (bsz, nc, CHUNK, N_ATTN_HEADS, HEAD_DIM)
    q = q.reshape(shp)
    k = k.reshape(shp)
    v = v.reshape(shp)
    pad = ((0, 0), (LEFT_CHUNKS, 0), (0, 0), (0, 0), (0, 0))
    kp = jnp.pad(k, pad)
    vp = jnp.pad(v, pad)
    kb = jnp.concatenate([kp[:, j:j + nc] for j in range(LEFT_CHUNKS + 1)], axis=2)
    vb = jnp.concatenate([vp[:, j:j + nc] for j in range(LEFT_CHUNKS + 1)], axis=2)
    scores = jnp.einsum('bcqhd,bckhd->bhcqk', q, kb).astype(jnp.float32) * (HEAD_DIM ** -0.5)
    qi = jnp.arange(CHUNK)[:, None]
    km = jnp.arange(BAND)[None, :]
    dist = LEFT_CHUNKS * CHUNK + qi - km
    idx = jnp.clip(dist, -(CHUNK - 1), MAX_REL) + (CHUNK - 1)
    bias = rel_table[:, idx].astype(jnp.float32)
    cidx = jnp.arange(nc)[:, None]
    band_chunk = (jnp.arange(BAND) // CHUNK)[None, :]
    valid = (cidx + band_chunk - LEFT_CHUNKS) >= 0
    scores = scores + bias[None, :, None]
    scores = jnp.where(valid[None, None, :, None, :], scores, NEG_INF)
    p = jax.nn.softmax(scores, axis=-1).astype(v.dtype)
    o = jnp.einsum('bhcqk,bckhd->bcqhd', p, vb)
    return o.reshape(bsz, s, D_ATTN)

def hybrid_mixer(x, w_in, b_in, rel_table, lconv_w, lconv_b, w_a, b_a, w_x, b_x, lam, w_out, b_out):
    z = x @ w_in + b_in
    q, k, v, xl, gl = jnp.split(
        z, [D_ATTN, 2 * D_ATTN, 3 * D_ATTN, 3 * D_ATTN + D_LRU], axis=-1)
    y_attn = chunk_band_attention(q, k, v, rel_table)
    xl = causal_dwconv(xl, lconv_w, lconv_b)
    y_lru = rg_lru(xl, w_a, b_a, w_x, b_x, lam) * jax.nn.gelu(gl)
    y = jnp.concatenate([y_attn, y_lru], axis=-1)
    return y @ w_out + b_out

def conv_gated_ffn(x, w_up, b_up, fconv_w, fconv_b, w_down, b_down):
    u = x @ w_up + b_up
    u = causal_dwconv(u, fconv_w, fconv_b)
    val, gate = jnp.split(u, 2, axis=-1)
    return (jax.nn.gelu(gate) * val) @ w_down + b_down

def setup_inputs(seed: int = 0) -> dict:
    key = jax.random.key(seed)
    ks = jax.random.split(key, 32)
    f32 = jnp.float32
    nrm = lambda k, shape, scale: jax.random.normal(k, shape, f32) * scale
    x = jax.random.normal(ks[0], (BATCH, SEQ, D_MODEL), f32)
    ln_in_g = 1.0 + nrm(ks[1], (D_MODEL,), 0.02)
    ln_in_b = nrm(ks[2], (D_MODEL,), 0.02)
    w_in = nrm(ks[3], (DEPTH, D_MODEL, D_IN), D_MODEL ** -0.5)
    col_scale = jnp.concatenate([jnp.ones((2 * D_ATTN,), f32), jnp.full((D_ATTN,), BETA, f32),
                                 jnp.ones((2 * D_LRU,), f32)])
    w_in = w_in * col_scale
    b_in = nrm(ks[4], (DEPTH, D_IN), 0.02)
    rel_bias = nrm(ks[5], (DEPTH, N_ATTN_HEADS, N_REL), 0.5)
    lru_conv_w = nrm(ks[6], (DEPTH, LRU_CONV_W, D_LRU), LRU_CONV_W ** -0.5)
    lru_conv_b = nrm(ks[7], (DEPTH, D_LRU), 0.02)
    lru_w_a = nrm(ks[8], (DEPTH, N_LRU_BLOCKS, LRU_BLOCK, LRU_BLOCK), LRU_BLOCK ** -0.5)
    lru_b_a = nrm(ks[9], (DEPTH, D_LRU), 0.02)
    lru_w_x = nrm(ks[10], (DEPTH, N_LRU_BLOCKS, LRU_BLOCK, LRU_BLOCK), LRU_BLOCK ** -0.5)
    lru_b_x = nrm(ks[11], (DEPTH, D_LRU), 0.02)
    a_c = jax.random.uniform(ks[12], (DEPTH, D_LRU), f32, 0.9, 0.999)
    a_base = a_c ** (1.0 / LRU_C)
    lru_lambda = jnp.log(a_base) - jnp.log1p(-a_base)
    w_out = nrm(ks[13], (DEPTH, D_MIX, D_MODEL), BETA * D_MIX ** -0.5)
    b_out = nrm(ks[14], (DEPTH, D_MODEL), 0.02)
    ln1_g = 1.0 + nrm(ks[15], (DEPTH, D_MODEL), 0.02)
    ln1_b = nrm(ks[16], (DEPTH, D_MODEL), 0.02)
    ffn_w_up = nrm(ks[17], (DEPTH, D_MODEL, 2 * D_FF), D_MODEL ** -0.5)
    ffn_b_up = nrm(ks[18], (DEPTH, 2 * D_FF), 0.02)
    ffn_conv_w = nrm(ks[19], (DEPTH, FFN_CONV_W, 2 * D_FF), FFN_CONV_W ** -0.5)
    ffn_conv_b = nrm(ks[20], (DEPTH, 2 * D_FF), 0.02)
    ffn_w_down = nrm(ks[21], (DEPTH, D_FF, D_MODEL), BETA * D_FF ** -0.5)
    ffn_b_down = nrm(ks[22], (DEPTH, D_MODEL), 0.02)
    ln2_g = 1.0 + nrm(ks[23], (DEPTH, D_MODEL), 0.02)
    ln2_b = nrm(ks[24], (DEPTH, D_MODEL), 0.02)
    return {"x": x, "ln_in_g": ln_in_g, "ln_in_b": ln_in_b, "w_in": w_in, "b_in": b_in,
            "rel_bias": rel_bias, "lru_conv_w": lru_conv_w, "lru_conv_b": lru_conv_b,
            "lru_w_a": lru_w_a, "lru_b_a": lru_b_a, "lru_w_x": lru_w_x, "lru_b_x": lru_b_x,
            "lru_lambda": lru_lambda, "w_out": w_out, "b_out": b_out,
            "ln1_g": ln1_g, "ln1_b": ln1_b, "ffn_w_up": ffn_w_up, "ffn_b_up": ffn_b_up,
            "ffn_conv_w": ffn_conv_w, "ffn_conv_b": ffn_conv_b, "ffn_w_down": ffn_w_down,
            "ffn_b_down": ffn_b_down, "ln2_g": ln2_g, "ln2_b": ln2_b}

def reference(x, ln_in_g, ln_in_b, w_in, b_in, rel_bias, lru_conv_w, lru_conv_b,
              lru_w_a, lru_b_a, lru_w_x, lru_b_x, lru_lambda, w_out, b_out,
              ln1_g, ln1_b, ffn_w_up, ffn_b_up, ffn_conv_w, ffn_conv_b, ffn_w_down,
              ffn_b_down, ln2_g, ln2_b):
    h = layer_norm(x, ln_in_g, ln_in_b)
    for l in range(DEPTH):
        mix = hybrid_mixer(h, w_in[l], b_in[l], rel_bias[l], lru_conv_w[l], lru_conv_b[l],
                           lru_w_a[l], lru_b_a[l], lru_w_x[l], lru_b_x[l], lru_lambda[l],
                           w_out[l], b_out[l])
        h = layer_norm(ALPHA * h + mix, ln1_g[l], ln1_b[l])
        ffn = conv_gated_ffn(h, ffn_w_up[l], ffn_b_up[l], ffn_conv_w[l], ffn_conv_b[l],
                             ffn_w_down[l], ffn_b_down[l])
        h = layer_norm(ALPHA * h + ffn, ln2_g[l], ln2_b[l])
    return h


_drawn_inputs = setup_inputs


def setup_inputs(seed=0):
    import zlib

    import numpy as np

    out = dict(_drawn_inputs(seed))
    spreads = {}
    factors = {'rel_bias': 7.673,
     'lru_b_a': 57.09,
     'lru_b_x': 36.398,
     'b_out': 3.313,
     'ln1_g': 2.733,
     'ln1_b': 2.741,
     'ffn_b_up': 6.373,
     'ffn_conv_b': 6.445,
     'ffn_b_down': 12.693,
     'ln2_g': 8.447,
     'ln2_b': 8.281}
    for name, (base, spread) in spreads.items():
        noise = np.random.default_rng([zlib.crc32(name.encode()), seed]).standard_normal(out[name].shape)
        drawn = base * np.exp(spread * noise) if base else spread * noise
        out[name] = __import__('jax').numpy.asarray(drawn.astype(out[name].dtype))
    for name, factor in factors.items():
        out[name] = (out[name] * factor).astype(out[name].dtype)
    return out
```

```python
from contextlib import ExitStack

import numpy as np

import concourse.bass as bass
from concourse import mybir

F32 = mybir.dt.float32
F32R = mybir.dt.float32r
ALU = mybir.AluOpType
ACT = mybir.ActivationFunctionType
AX = mybir.AxisListType

P = 128
T, D = 2048, 1024
KD = D // P
DA = 512
NA = DA // P
HEADS, HD = 8, 64
CHUNK, LEFT, MAX_REL = 64, 8, 128
N_REL = CHUNK - 1 + MAX_REL + 1
FF = 2816
NF = FF // P
TT = T // P
BLK = 512
NB = T // BLK
TPB = BLK // P
EPS = 1e-5
ALPHA = 2.0 ** 0.25
SCALE = HD ** -0.5
NEG = -1e30
LRU_C = 8.0
CW, FW = 4, 3
CREDITS = 2
NEAR = 2 * P
BIAS_EXT = NEAR + P - 1


def ticks(eng, count, depth, body):
    first = depth + depth % 2
    last = count - count % 2

    def fixed(n):
        return lambda k: divmod(n - k, 2) if 0 <= n - k < count else None

    for n in range(first):
        body(fixed(n))
    with eng.Fori(first // 2, last // 2) as g:
        for u in range(2):
            body(lambda k, u=u: (g + (u - k) // 2, (u - k) % 2))
    for n in range(last, count + depth - 1):
        body(fixed(n))


def whole(eng, top, *waits):
    for _, value in waits:
        if not isinstance(value, int):
            eng.compute_val(value)
    eng.wait_ge(top.started, 1)
    for sem, value in waits:
        eng.wait_ge(sem, value)


def rounds(eng, count, body):
    with eng.Fori(0, count - 1) as t:
        body(t)
    body(count - 1)


def three_passes(pe, out, w_hi, w_lo, x_hi, x_lo, start, stop):
    pe.matmul(out, w_hi, x_hi, start=start, stop=False)
    pe.matmul(out, w_hi, x_lo, start=False, stop=False)
    return pe.matmul(out, w_lo, x_hi, start=False, stop=stop)


def token_major(pe, out, x_hi, x_lo, w_hi, w_lo, start, stop):
    halves = [slice(0, BLK), slice(BLK, D)]
    for x, w, first in ((x_hi, w_hi, start), (x_hi, w_lo, False), (x_lo, w_hi, False)):
        for half in halves:
            last = pe.matmul(out[:, half], x, w[:, half], start=first, stop=stop and x is x_lo)
    return last


class Tools:

    def __init__(self, nc, stack):
        self.nc, self.stack = nc, stack

    def sem(self, name, n=None):
        one = lambda x: self.stack.enter_context(self.nc.semaphore(x))
        return one(name) if n is None else [one(f"{name}_{i}") for i in range(n)]

    def phase(self):
        return Tools(self.nc, ExitStack())

    def sb(self, name, shape, dt=F32):
        return self.stack.enter_context(self.nc.sbuf_tensor(name, [P, *shape], dt))

    def ps(self, name, cols):
        return self.stack.enter_context(self.nc.psum_tensor(name, [P, cols], F32))


def f32(x):
    return x.bitcast(F32)


def identity(nc, pool, ident, sem):
    nc.gpsimd.memset(ident[:, :], 0.0).then_inc(sem, 1)
    pool.wait_ge(sem, 1)
    nc.gpsimd.affine_select(out=ident[:, :], in_=ident[:, :], compare_op=ALU.not_equal, fill=1.0,
                            base=0, pattern=[[-1, P]], channel_multiplier=1).then_inc(sem, 1)


def phase1(nc, top, io, scr):
    m = top.phase()
    x_sb = m.sb("x_sb", [2, D])
    h_sb = m.sb("h_sb", [2, D])
    hT_hi = m.sb("hT_hi", [2, KD, P], F32R)
    hT_lo = m.sb("hT_lo", [2, KD, P], F32R)
    wv_raw = m.sb("wv_raw", [KD, DA])
    wv_hi = m.sb("wv_hi", [KD, DA], F32R)
    wv_lo = m.sb("wv_lo", [KD, DA], F32R)
    v_hi = m.sb("v_hi", [2, DA], F32R)
    v_lo = m.sb("v_lo", [2, DA], F32R)
    gain = m.sb("ln_in_gain", [D])
    shift = m.sb("ln_in_shift", [D])
    ident = m.sb("ident1", [P])
    stats = m.sb("stats1", [2, 12])
    mean_var = m.sb("mean_var1", [2, 2])
    var_eps = m.sb("var_eps1", [2, 1])
    minus_half = m.sb("minus_half1", [1])
    rstd = m.sb("rstd1", [2, 1])
    tp = [m.ps(f"h_transposed{i}", D) for i in range(2)]
    vp = [m.ps(f"v_psum{i}", DA) for i in range(2)]

    x_loaded, h_stored, hT_stored, v_stored = (top.sem(n, 2) for n in (
        "x_loaded", "h_stored", "hT_stored", "v_stored"))
    (rows_loaded, wv_loaded, const1, stats_step, var_ready, rstd_ready, normed, gained,
     h_ready, transposed, hhi_ready, hlo_ready, wvhi_ready, wvlo_ready, v_ready, vhi_ready,
     vlo_ready) = map(top.sem, (
        "rows_loaded", "wv_loaded", "const1", "stats_step", "var_ready", "rstd_ready",
        "normed", "gained", "h_ready", "transposed", "hhi_ready", "hlo_ready", "wvhi_ready",
        "wvlo_ready", "v_ready", "vhi_ready", "vlo_ready"))
    bias_stored, rel_in, ext_ready = (top.sem(n) for n in ("bias_stored", "rel_in", "ext_ready"))
    ext_sb = m.sb("bias_ext_sb", [BIAS_EXT])
    DEPTH1 = 6
    LOAD, STATS, NORM, TURN, VALUE, STORE_V = range(DEPTH1)

    with nc.Block() as block:
        @block.sync
        def _(sp):
            for s in (normed, transposed, hlo_ready, vlo_ready):
                sp.sem_inc(s, CREDITS)
            for u in range(2):
                for s in (h_stored, hT_stored, v_stored):
                    sp.sem_inc(s[u], 16)
            ext = scr["bias_ext"]
            sp.wait_ge(ext_ready, 1)
            sp.dma_start(ext_sb[0:HEADS, P - 1:P - 1 + N_REL], io["rel_bias_reversed"]
                         ).then_inc(rel_in, 16)
            sp.wait_ge(ext_ready, 2)
            sp.dma_start(ext, ext_sb[0:HEADS, :]).then_inc(bias_stored, 16)
            sp.wait_ge(bias_stored, 16)
            sp.dma_start(scr["bias_rows"].rearrange("p h m -> p (h m)"),
                         ext.rearrange("h m -> (h m)").partition_broadcast(P)).then_inc(bias_stored, 16)

            def body(at):
                if tile := at(LOAD):
                    j, u = tile
                    t = 2 * j + u
                    whole(sp, top, (normed, t + 1))
                    sp.dma_start(x_sb[:, u, :], io["x"][bass.ts(t, P), :]).then_inc(x_loaded[u], 16)
                if tile := at(TURN):
                    j, u = tile
                    t = 2 * j + u
                    whole(sp, top, (h_ready, t + 1))
                    sp.dma_start(scr["h0"][bass.ts(t, P), :], h_sb[:, u, :]).then_inc(h_stored[u], 16)
                if tile := at(VALUE):
                    j, u = tile
                    t = 2 * j + u
                    whole(sp, top, (hlo_ready, t + 1 + CREDITS))
                    for part, src in ((0, hT_hi), (1, hT_lo)):
                        sp.dma_start(scr["h0T"][part, :, :, bass.ts(t, P)].rearrange("k p t -> p k t"),
                                     f32(src[:, u, :, :])).then_inc(hT_stored[u], 16)
                if tile := at(STORE_V):
                    j, u = tile
                    t = 2 * j + u
                    whole(sp, top, (vlo_ready, t + 1 + CREDITS))
                    for part, src in ((0, v_hi), (1, v_lo)):
                        sp.dma_start(scr["v"][part, bass.ts(t, P), :],
                                     f32(src[:, u, :])).then_inc(v_stored[u], 16)

            ticks(sp, TT, DEPTH1, body)
            for u in range(2):
                sp.wait_ge(h_stored[u], 16 + 16 * TT // 2)
                sp.wait_ge(hT_stored[u], 16 + 32 * TT // 2)
                sp.wait_ge(v_stored[u], 16 + 32 * TT // 2)
            sp.wait_ge(bias_stored, 32)

        @block.gpsimd
        def _(pool):
            identity(nc, pool, ident, const1)
            nc.gpsimd.memset(minus_half[:, :], -0.5).then_inc(const1, 1)
            pool.wait_ge(const1, 3)
            pool.wait_ge(rows_loaded, 32)

            def body(at):
                if tile := at(STATS):
                    j, u = tile
                    t = 2 * j + u
                    pool.wait_ge(var_ready, t + 1)
                    pool.wait_ge(normed, t + 1)
                    nc.gpsimd.tensor_tensor(out=rstd[:, u, :], in0=var_eps[:, u, :],
                                            in1=minus_half[:, :], op=ALU.pow).then_inc(rstd_ready, 1)
                if tile := at(NORM):
                    j, u = tile
                    t = 2 * j + u
                    pool.wait_ge(gained, t + 1)
                    nc.gpsimd.tensor_tensor(out=h_sb[:, u, :], in0=h_sb[:, u, :], in1=shift[:, :],
                                            op=ALU.add).then_inc(h_ready, 1)

            ticks(pool, TT, DEPTH1, body)

        @block.scalar
        def _(act):
            act.dma_start(gain[:, :], io["ln_in_g"].partition_broadcast(P)).then_inc(rows_loaded, 16)
            act.dma_start(shift[:, :], io["ln_in_b"].partition_broadcast(P)).then_inc(rows_loaded, 16)
            act.dma_start(wv_raw[:, :, :],
                          io["w_in"][:, 2 * DA:3 * DA].rearrange("(k p) n -> p k n", p=P)
                          ).then_inc(wv_loaded, 16)
            act.wait_ge(wv_loaded, 16)
            for k in range(KD):
                nc.scalar.activation(wv_hi[:, k, :], wv_raw[:, k, :], ACT.Copy).then_inc(wvhi_ready, 1)

            def body(at):
                if tile := at(TURN):
                    j, u = tile
                    t = 2 * j + u
                    act.wait_ge(transposed, t + 1 + CREDITS)
                    act.wait_ge(hT_stored[u], 16 + 32 * j)
                    act.wait_ge(vlo_ready, t + 1)
                    nc.scalar.activation(hT_hi[:, u, :, :].rearrange("p k t -> p (k t)"), tp[u][:, :],
                                         ACT.Copy).then_inc(hhi_ready, 1)
                if tile := at(VALUE):
                    j, u = tile
                    t = 2 * j + u
                    act.wait_ge(v_ready, t + 1)
                    act.wait_ge(v_stored[u], 16 + 32 * j)
                    nc.scalar.activation(v_hi[:, u, :], vp[u][:, :], ACT.Copy).then_inc(vhi_ready, 1)

            ticks(act, TT, DEPTH1, body)

        @block.vector
        def _(dve):
            nc.vector.memset(ext_sb[0:HEADS, :], 0.0).then_inc(ext_ready, 1)
            dve.wait_ge(rel_in, 16)
            nc.vector.tensor_scalar(ext_sb[0:HEADS, 0:P - 1], ext_sb[0:HEADS, 0:P - 1],
                                    ext_sb[0:HEADS, P - 1:P], None, ALU.add).then_inc(ext_ready, 1)
            for k in range(KD):
                dve.wait_ge(wvhi_ready, k + 1)
                nc.vector.tensor_tensor(out=wv_lo[:, k, :], in0=wv_raw[:, k, :],
                                        in1=f32(wv_hi[:, k, :]), op=ALU.subtract).then_inc(wvlo_ready, 1)
            dve.wait_ge(rows_loaded, 32)

            def body(at):
                if tile := at(STATS):
                    j, u = tile
                    t = 2 * j + u
                    dve.wait_ge(x_loaded[u], 16 * (j + 1))
                    nc.vector.bn_stats(stats[:, u, 0:6], x_sb[:, u, 0:D // 2])
                    nc.vector.bn_stats(stats[:, u, 6:12], x_sb[:, u, D // 2:D]).then_inc(stats_step, 1)
                    whole(dve, top, (stats_step, 2 * t + 1))
                    nc.vector.bn_aggr(mean_var[:, u, :], stats[:, u, :]).then_inc(stats_step, 1)
                    dve.wait_ge(stats_step, 2 * t + 2)
                    nc.vector.tensor_scalar(var_eps[:, u, :], mean_var[:, u, 1:2], EPS, None,
                                            ALU.add).then_inc(var_ready, 1)
                if tile := at(NORM):
                    j, u = tile
                    t = 2 * j + u
                    dve.wait_ge(rstd_ready, t + 1)
                    dve.wait_ge(transposed, t + 1)
                    dve.wait_ge(h_stored[u], 16 * (j + 1))
                    nc.vector.tensor_scalar(h_sb[:, u, :], x_sb[:, u, :], mean_var[:, u, 0:1],
                                            rstd[:, u, :], ALU.subtract, ALU.mult).then_inc(normed, 1)
                    dve.wait_ge(normed, t + 1 + CREDITS)
                    nc.vector.tensor_tensor(out=h_sb[:, u, :], in0=h_sb[:, u, :], in1=gain[:, :],
                                            op=ALU.mult).then_inc(gained, 1)
                if tile := at(TURN):
                    j, u = tile
                    t = 2 * j + u
                    dve.wait_ge(hhi_ready, t + 1)
                    nc.vector.tensor_tensor(out=hT_lo[:, u, :, :].rearrange("p k t -> p (k t)"),
                                            in0=tp[u][:, :],
                                            in1=f32(hT_hi[:, u, :, :]).rearrange("p k t -> p (k t)"),
                                            op=ALU.subtract).then_inc(hlo_ready, 1)
                if tile := at(VALUE):
                    j, u = tile
                    t = 2 * j + u
                    dve.wait_ge(vhi_ready, t + 1)
                    nc.vector.tensor_tensor(out=v_lo[:, u, :], in0=vp[u][:, :], in1=f32(v_hi[:, u, :]),
                                            op=ALU.subtract).then_inc(vlo_ready, 1)

            ticks(dve, TT, DEPTH1, body)

        @block.tensor
        def _(pe):
            pe.wait_ge(const1, 2)

            def body(at):
                if tile := at(TURN):
                    j, u = tile
                    t = 2 * j + u
                    pe.wait_ge(h_ready, t + 1)
                    pe.wait_ge(hlo_ready, t + 1)
                    for k in range(KD):
                        last = nc.tensor.transpose(tp[u][:, bass.ts(k, P)], h_sb[:, u, bass.ts(k, P)],
                                                   ident[:, :])
                    last.then_inc(transposed, 1)
                if tile := at(VALUE):
                    j, u = tile
                    t = 2 * j + u
                    if isinstance(t, int) and t == 0:
                        pe.wait_ge(wvlo_ready, KD)
                    pe.wait_ge(hlo_ready, t + 1 + CREDITS)
                    pe.wait_ge(vlo_ready, t + 1)
                    for k in range(KD):
                        last = three_passes(nc.tensor, vp[u][:, :], hT_hi[:, u, k, :], hT_lo[:, u, k, :],
                                            wv_hi[:, k, :], wv_lo[:, k, :], k == 0, k == KD - 1)
                    last.then_inc(v_ready, 1)

            ticks(pe, TT, DEPTH1, body)
    m.stack.close()


def phase2(nc, top, io, scr):
    m = top.phase()
    hT_hi = m.sb("hT_hi2", [KD, T], F32R)
    hT_lo = m.sb("hT_lo2", [KD, T], F32R)
    w_raw = m.sb("w_raw2", [2, KD, P])
    w_hi = m.sb("w_hi2", [2, KD, P], F32R)
    w_lo = m.sb("w_lo2", [2, KD, P], F32R)
    xl = m.sb("xl", [CW - 1 + T])
    gl = m.sb("gelu_gate", [T])
    xc = m.sb("conv_out", [T])
    xc_hi = m.sb("xc_hi", [2, BLK], F32R)
    xc_lo = m.sb("xc_lo", [2, BLK], F32R)
    decay = m.sb("decay", [2, BLK])
    mult = m.sb("mult", [2, BLK])
    state = m.sb("state", [2, BLK])
    o_hi = m.sb("o_hi2", [2, BLK], F32R)
    o_lo = m.sb("o_lo2", [2, BLK], F32R)
    gw_raw = m.sb("gw_raw", [2, P])
    gw_hi = m.sb("gw_hi", [2, P], F32R)
    gw_lo = m.sb("gw_lo", [2, P], F32R)
    b_in = m.sb("b_in", [3 * NA + 2 * NA])
    vecs = m.sb("lru_vectors", [9, NA])
    TAP, CONV_B, B_A, B_X, LAMBDA, RATE = 0, 4, 5, 6, 7, 8
    sp_tmp = m.sb("softplus_tmp", [4, NA])
    mm = [m.ps(f"mm2_{i}", BLK) for i in range(2)]
    gate_r = [m.ps(f"gate_r{i}", BLK) for i in range(2)]
    gate_i = [m.ps(f"gate_i{i}", BLK) for i in range(2)]

    hT_in = top.sem("hT_in", NB)
    w_in, o_stored, evac = (top.sem(n, 2) for n in ("w_loaded2", "o_stored2", "evac2"))
    (consts_in, gw_in, gwhi, gw_split, whi, w_split, mm_ready, xl_ready, conv_step, conv_done, xchi,
     xclo, gates_ready, tanh_done, log_ready, exp_done, squared, m2_ready, sqrt_done, u_ready, h_ready,
     gl_free, y_ready, hi_ready, soft, soft_act, pad_ready) = (top.sem(n + "_2") for n in (
        "consts_in", "gw_in", "gwhi", "gw_split", "whi", "w_split", "mm_ready", "xl_ready",
        "conv_step", "conv_done", "xchi", "xclo", "gates_ready", "tanh_done", "log_ready", "exp_done",
        "squared", "m2_ready", "sqrt_done", "u_ready", "h_ready", "gl_free", "y_ready", "hi_ready",
        "soft", "soft_act", "pad_ready"))
    GATE, XIN, QUERY, KEY = range(4)
    CHUNK_COL = {GATE: 3 * DA + DA, XIN: 3 * DA, QUERY: 0, KEY: DA}
    NCH = 4 * NA
    ITEMS = 12
    MM0 = 2 * NB
    A, B, C, DD = "gates to log decay", "decay and input", "scan", "split"
    BESIDE = {(XIN, 3): [(A, 0)], (QUERY, 0): [(B, 0), (A, 1)], (QUERY, 1): [(C, 0), (B, 1)],
              (QUERY, 2): [(DD, 0), (C, 1)], (QUERY, 3): [(DD, 1), (A, 2)], (KEY, 0): [(B, 2), (A, 3)],
              (KEY, 1): [(C, 2), (B, 3)], (KEY, 2): [(DD, 2), (C, 3)], (KEY, 3): [(DD, 3)]}
    GATES = {(XIN, 2): 0, (XIN, 3): 1, (QUERY, 2): 2, (QUERY, 3): 3}
    XC_SPLIT = {(XIN, 1): 0, (XIN, 2): 1, (QUERY, 0): 2, (QUERY, 1): 3}
    ORDER = [(QUERY, 0), (QUERY, 1), (QUERY, 2), (DD, 0), (QUERY, 3), (DD, 1), (KEY, 0), (KEY, 1),
             (KEY, 2), (DD, 2), (KEY, 3), (DD, 3)]

    def item_of(chunk, b):
        return ORDER.index((chunk, b))

    with nc.Block() as block:
        @block.sync
        def _(sp):
            for s, n in ((w_split, CREDITS), (mm_ready, MM0), (conv_done, 1), (gl_free, NB),
                         (u_ready, CREDITS), (gw_split, 1), (gates_ready, CREDITS),
                         (h_ready, CREDITS)):
                sp.sem_inc(s, n)
            for u in range(2):
                sp.sem_inc(o_stored[u], 16)
                sp.sem_inc(evac[u], 1)

            def load(n, t, c):
                whole(sp, top, (w_split, n + 1))
                cols = io["w_in"][:, bass.ds(t * P + CHUNK_COL[c], P)]
                sp.dma_start(w_raw[:, c % 2, :, :], cols.rearrange("(k p) n -> p k n", p=P)
                             ).then_inc(w_in[c % 2], 16)

            load(0, 0, GATE)
            for part, dst in ((0, hT_hi), (1, hT_lo)):
                sp.dma_start(f32(dst[:, :, 0:BLK]),
                             scr["h0T"][part, :, :, 0:BLK].rearrange("k p t -> p k t")
                             ).then_inc(hT_in[0], 16)
            load(1, 0, XIN)
            for b in range(1, NB):
                for part, dst in ((0, hT_hi), (1, hT_lo)):
                    sp.dma_start(f32(dst[:, :, bass.ts(b, BLK)]),
                                 scr["h0T"][part, :, :, bass.ts(b, BLK)].rearrange("k p t -> p k t")
                                 ).then_inc(hT_in[b], 16)

            def body(t):
                last = isinstance(t, int)

                def store(name, chunk, b, k0):
                    i = item_of(chunk, b)
                    if chunk == DD:
                        whole(sp, top, (gl_free, NB * t + b + 1 + NB))
                    else:
                        whole(sp, top, (evac[b % 2], 1 + 8 * t + 2 * chunk + b // 2 + 1))
                    for part, src in ((0, o_hi), (1, o_lo)):
                        sp.dma_start(scr[name][part, bass.ds(t + k0, 1), :, bass.ts(b, BLK)]
                                     .rearrange("k p t -> p (k t)"),
                                     f32(src[:, i % 2, :])).then_inc(o_stored[i % 2], 16)

                whole(sp, top, (gw_split, t + 1))
                sp.dma_start(gw_raw[:, :, :], io["gate_w"][bass.ds(t, 1), :, :, :]
                             .rearrange("t p g n -> p (t g) n")).then_inc(gw_in, 16)
                for c in range(4):
                    if not (last and c >= 2):
                        load(4 * t + c + 2, t + (c + 2) // 4, (c + 2) % 4)
                    for b in range(NB):
                        if c == QUERY:
                            store("q", QUERY, b, 0)
                        if c == KEY:
                            store("k", KEY, b, 0)
                        for stage, sb in BESIDE.get((c, b), ()):
                            if stage == DD:
                                store("yT", DD, sb, NA)

            rounds(sp, NA, body)
            for u in range(2):
                sp.wait_ge(o_stored[u], 16 + 32 * ITEMS * NA // 2)

        @block.gpsimd
        def _(pool):
            nc.gpsimd.memset(xl[:, 0:CW - 1], 0.0).then_inc(pad_ready, 1)

        @block.scalar
        def _(act):
            act.dma_start(b_in[:, :], io["b_in"]).then_inc(consts_in, 16)
            act.dma_start(vecs[:, 0:8, :], io["lru_vectors"]).then_inc(consts_in, 16)
            act.wait_ge(soft, 1)
            nc.scalar.activation(sp_tmp[:, 1, :], sp_tmp[:, 0, :], ACT.Exp, scale=-1.0).then_inc(soft_act, 1)
            act.wait_ge(consts_in, 32)

            def hi(t, c):
                act.wait_ge(w_in[c % 2], 32 * t + 16 * (c // 2 + 1))
                act.wait_ge(mm_ready, 16 * t + 4 * c - 4 + MM0)
                nc.scalar.activation(w_hi[:, c % 2, :, :].rearrange("p k n -> p (k n)"),
                                     w_raw[:, c % 2, :, :].rearrange("p k n -> p (k n)"),
                                     ACT.Copy).then_inc(whi, 1)

            hi(0, GATE)

            def body(t):
                last = isinstance(t, int)

                def split_hi(chunk, b, src, bias, source_ready):
                    i = item_of(chunk, b)
                    whole(act, top, source_ready,
                          (o_stored[i % 2], 16 + 32 * (ITEMS // 2 * t + i // 2)))
                    nc.scalar.activation(o_hi[:, i % 2, :], src, ACT.Identity, bias=bias
                                         ).then_inc(hi_ready, 1)

                for c in range(4):
                    for b in range(NB):
                        product = (mm_ready, 16 * t + 4 * c + b + 1 + MM0)
                        if c == GATE:
                            whole(act, top, product, (gl_free, NB * t + b + 1))
                            nc.scalar.activation(gl[:, bass.ts(b, BLK)], mm[b % 2][:, :],
                                                 ACT.Gelu_apprx_tanh,
                                                 bias=b_in[:, bass.ds(t + 4 * NA, 1)]
                                                 ).then_inc(evac[b % 2], 1)
                        if c == XIN:
                            whole(act, top, product, (conv_done, NB * t + 1))
                            nc.scalar.activation(xl[:, bass.ds(CW - 1 + b * BLK, BLK)], mm[b % 2][:, :],
                                                 ACT.Identity, bias=b_in[:, bass.ds(t + 3 * NA, 1)]
                                                 ).then_inc(evac[b % 2], 1)
                        if c == QUERY:
                            split_hi(QUERY, b, mm[b % 2][:, :], b_in[:, bass.ds(t, 1)], product)
                        if c == KEY:
                            split_hi(KEY, b, mm[b % 2][:, :], b_in[:, bass.ds(t + NA, 1)], product)
                        if b == 0 and not (last and c == KEY):
                            hi(t + (c + 1) // 4, (c + 1) % 4)
                        if c == XIN and b == 0:
                            act.wait_ge(gw_in, 16 * t + 16)
                            act.wait_ge(gates_ready, NB * t + CREDITS)
                            nc.scalar.activation(gw_hi[:, :, :], gw_raw[:, :, :], ACT.Copy
                                                 ).then_inc(gwhi, 1)
                        if (c, b) in XC_SPLIT:
                            sb = XC_SPLIT[c, b]
                            act.wait_ge(conv_done, NB * t + sb + 2)
                            act.wait_ge(gates_ready, NB * t + sb + 1)
                            nc.scalar.activation(xc_hi[:, sb % 2, :], xc[:, bass.ts(sb, BLK)], ACT.Copy
                                                 ).then_inc(xchi, 1)
                        for stage, sb in BESIDE.get((c, b), ()):
                            s = sb % 2
                            if stage == A:
                                whole(act, top, (gates_ready, NB * t + sb + 1 + CREDITS))
                                nc.scalar.activation(gate_r[s][:, :], gate_r[s][:, :], ACT.Tanh, scale=0.5,
                                                     bias=vecs[:, B_A, bass.ds(t, 1)]).then_inc(tanh_done, 1)
                                nc.scalar.activation(gate_i[s][:, :], gate_i[s][:, :], ACT.Tanh, scale=0.5,
                                                     bias=vecs[:, B_X, bass.ds(t, 1)]).then_inc(tanh_done, 1)
                            if stage == B:
                                act.wait_ge(log_ready, NB * t + sb + 1)
                                act.wait_ge(h_ready, NB * t + sb + 1)
                                nc.scalar.activation(decay[:, s, :], gate_r[s][:, :], ACT.Exp
                                                     ).then_inc(exp_done, 1)
                                act.wait_ge(exp_done, 2 * (NB * t + sb) + 1)
                                nc.scalar.activation(gate_r[s][:, :], gate_r[s][:, :], ACT.Tanh, scale=-1.0
                                                     ).then_inc(exp_done, 1)
                            if stage == C:
                                act.wait_ge(m2_ready, NB * t + sb + 1)
                                nc.scalar.activation(mult[:, s, :], mult[:, s, :], ACT.Sqrt, scale=0.25
                                                     ).then_inc(sqrt_done, 1)
                            if stage == DD:
                                split_hi(DD, sb, gl[:, bass.ts(sb, BLK)], 0.0,
                                         (y_ready, NB * t + sb + 1))

            rounds(act, NA, body)

        @block.vector
        def _(dve):
            dve.wait_ge(consts_in, 32)
            lam, e, z, z2, acc = (vecs[:, LAMBDA, :], sp_tmp[:, 1, :], sp_tmp[:, 2, :], sp_tmp[:, 3, :],
                                  vecs[:, RATE, :])
            nc.vector.scalar_tensor_tensor(sp_tmp[:, 0, :], lam, -1.0, lam, ALU.mult, ALU.max
                                           ).then_inc(soft, 1)
            dve.wait_ge(soft_act, 1)
            n = 1

            def chain(instruction):
                nonlocal n
                instruction.then_inc(soft, 1)
                n += 1
                dve.wait_ge(soft, n)

            chain(nc.vector.tensor_scalar(z2, e, 2.0, None, ALU.add))
            chain(nc.vector.reciprocal(z, z2))
            chain(nc.vector.tensor_tensor(out=z, in0=z, in1=e, op=ALU.mult))
            chain(nc.vector.tensor_tensor(out=z2, in0=z, in1=z, op=ALU.mult))
            chain(nc.vector.tensor_scalar(acc, z2, 1.0 / 17, 1.0 / 15, ALU.mult, ALU.add))
            for d in (13, 11, 9, 7, 5, 3, 1):
                chain(nc.vector.tensor_tensor(out=acc, in0=acc, in1=z2, op=ALU.mult))
                chain(nc.vector.tensor_scalar(acc, acc, 1.0 / d, None, ALU.add))
            chain(nc.vector.tensor_tensor(out=acc, in0=acc, in1=z, op=ALU.mult))
            chain(nc.vector.tensor_scalar(z, lam, -0.5, 0.0, ALU.mult, ALU.max))
            chain(nc.vector.tensor_tensor(out=acc, in0=acc, in1=z, op=ALU.add))
            chain(nc.vector.tensor_scalar(acc, acc, -LRU_C, None, ALU.mult))
            chain(nc.vector.tensor_scalar(vecs[:, B_A:B_X + 1, :], vecs[:, B_A:B_X + 1, :], 0.5, None,
                                          ALU.mult))
            dve.wait_ge(pad_ready, 1)

            def lo(t, c):
                dve.wait_ge(whi, 4 * t + c + 1)
                nc.vector.tensor_tensor(out=w_lo[:, c % 2, :, :].rearrange("p k n -> p (k n)"),
                                        in0=w_raw[:, c % 2, :, :].rearrange("p k n -> p (k n)"),
                                        in1=f32(w_hi[:, c % 2, :, :]).rearrange("p k n -> p (k n)"),
                                        op=ALU.subtract).then_inc(w_split, 1)

            lo(0, GATE)

            def body(t):
                last = isinstance(t, int)
                vec = lambda row: vecs[:, row, bass.ds(t, 1)]

                def split_lo(chunk, b, src, bias):
                    i = item_of(chunk, b)
                    dve.wait_ge(hi_ready, ITEMS * t + i + 1)
                    return nc.vector.scalar_tensor_tensor(o_lo[:, i % 2, :], src, bias,
                                                          f32(o_hi[:, i % 2, :]), ALU.add, ALU.subtract)

                for c in range(4):
                    for b in range(NB):
                        if c == QUERY:
                            split_lo(QUERY, b, mm[b % 2][:, :], b_in[:, bass.ds(t, 1)]
                                     ).then_inc(evac[b % 2], 1)
                        if c == KEY:
                            split_lo(KEY, b, mm[b % 2][:, :], b_in[:, bass.ds(t + NA, 1)]
                                     ).then_inc(evac[b % 2], 1)
                        if b == 0 and not (last and c == KEY):
                            lo(t + (c + 1) // 4, (c + 1) % 4)
                        if c == XIN:
                            if b == 0:
                                dve.wait_ge(gwhi, t + 1)
                                nc.vector.tensor_tensor(out=gw_lo[:, :, :], in0=gw_raw[:, :, :],
                                                        in1=f32(gw_hi[:, :, :]), op=ALU.subtract
                                                        ).then_inc(gw_split, 1)
                            dve.wait_ge(evac[b % 2], 1 + 8 * t + 2 + b // 2 + 1)
                            out = xc[:, bass.ts(b, BLK)]
                            nc.vector.tensor_scalar(out, xl[:, bass.ds(b * BLK, BLK)], vec(TAP),
                                                    vec(CONV_B), ALU.mult, ALU.add).then_inc(conv_step, 1)
                            for k in range(1, CW):
                                dve.wait_ge(conv_step, (CW - 1) * (NB * t + b) + k)
                                nc.vector.scalar_tensor_tensor(
                                    out, xl[:, bass.ds(b * BLK + k, BLK)], vec(TAP + k), out,
                                    ALU.mult, ALU.add).then_inc(conv_step if k < CW - 1 else conv_done, 1)
                        if (c, b) in XC_SPLIT:
                            sb = XC_SPLIT[c, b]
                            dve.wait_ge(xchi, NB * t + sb + 1)
                            nc.vector.tensor_tensor(out=xc_lo[:, sb % 2, :], in0=xc[:, bass.ts(sb, BLK)],
                                                    in1=f32(xc_hi[:, sb % 2, :]), op=ALU.subtract
                                                    ).then_inc(xclo, 1)
                        for stage, sb in BESIDE.get((c, b), ()):
                            s = sb % 2
                            i = NB * t + sb
                            if stage == A:
                                dve.wait_ge(tanh_done, 2 * i + 2)
                                nc.vector.tensor_scalar(gate_r[s][:, :], gate_r[s][:, :], 1.0, vec(RATE),
                                                        ALU.add, ALU.mult).then_inc(log_ready, 1)
                                nc.vector.scalar_tensor_tensor(gate_i[s][:, :], gate_i[s][:, :], 1.0,
                                                               xc[:, bass.ts(sb, BLK)], ALU.add, ALU.mult
                                                               )
                            if stage == B:
                                dve.wait_ge(exp_done, 2 * i + 2)
                                nc.vector.tensor_tensor(out=mult[:, s, :], in0=decay[:, s, :],
                                                        in1=decay[:, s, :], op=ALU.mult).then_inc(squared, 1)
                                dve.wait_ge(squared, i + 1)
                                nc.vector.scalar_tensor_tensor(mult[:, s, :], mult[:, s, :], 1.0,
                                                               gate_r[s][:, :], ALU.add, ALU.mult
                                                               ).then_inc(m2_ready, 1)
                            if stage == C:
                                dve.wait_ge(sqrt_done, i + 1)
                                nc.vector.tensor_tensor(out=mult[:, s, :], in0=gate_i[s][:, :],
                                                        in1=mult[:, s, :], op=ALU.mult).then_inc(u_ready, 1)
                                dve.wait_ge(u_ready, i + 1 + CREDITS)
                                before = 0.0 if sb == 0 else state[:, 1 - s, BLK - 1:BLK]
                                nc.vector.tensor_tensor_scan(state[:, s, :], decay[:, s, :], mult[:, s, :],
                                                             before, ALU.mult, ALU.add).then_inc(h_ready, 1)
                                dve.wait_ge(h_ready, i + 1 + CREDITS)
                                nc.vector.tensor_tensor(out=gl[:, bass.ts(sb, BLK)], in0=state[:, s, :],
                                                        in1=gl[:, bass.ts(sb, BLK)], op=ALU.mult
                                                        ).then_inc(y_ready, 1)
                            if stage == DD:
                                split_lo(DD, sb, gl[:, bass.ts(sb, BLK)], 0.0).then_inc(gl_free, 1)

            rounds(dve, NA, body)

        @block.tensor
        def _(pe):
            def body(t):
                for c in range(4):
                    pe.wait_ge(w_split, 4 * t + c + 1 + CREDITS)
                    for b in range(NB):
                        if isinstance(t, int) is False and c == GATE:
                            pe.wait_ge(hT_in[b], 32)
                        pe.wait_ge(evac[b % 2], 8 * t + 2 * c + b // 2 + 1)
                        for k in range(KD):
                            last = three_passes(nc.tensor, mm[b % 2][:, :], w_hi[:, c % 2, k, :],
                                                w_lo[:, c % 2, k, :], hT_hi[:, k, bass.ts(b, BLK)],
                                                hT_lo[:, k, bass.ts(b, BLK)], k == 0, k == KD - 1)
                        last.then_inc(mm_ready, 1)
                        if (c, b) in GATES:
                            gb = GATES[c, b]
                            s = gb % 2
                            pe.wait_ge(xclo, NB * t + gb + 1)
                            pe.wait_ge(gw_split, t + 2)
                            pe.wait_ge(u_ready, NB * t + gb + 1)
                            three_passes(nc.tensor, gate_r[s][:, :], gw_hi[:, 0, :], gw_lo[:, 0, :],
                                         xc_hi[:, s, :], xc_lo[:, s, :], True, True)
                            three_passes(nc.tensor, gate_i[s][:, :], gw_hi[:, 1, :], gw_lo[:, 1, :],
                                         xc_hi[:, s, :], xc_lo[:, s, :], True, True
                                         ).then_inc(gates_ready, 1)

            rounds(pe, NA, body)
    m.stack.close()


def sweep(eng, rounds_, steps, depth, body):
    def fixed(n):
        return lambda k: divmod(n - k, steps) if 0 <= n - k < rounds_ * steps else None

    for n in range(depth):
        body(fixed(n))
    with eng.Fori(0, rounds_ - 1) as g:
        for n in range(depth, depth + steps):
            body(lambda k, n=n: (g + (n - k) // steps, (n - k) % steps))
    for n in range(depth + steps * (rounds_ - 1), depth + steps * rounds_):
        body(fixed(n))


def phase3(nc, top, io, scr):
    m = top.phase()
    q_hi, q_lo, k_hi, k_lo = (m.sb(n, [T], F32R) for n in ("q_hi", "q_lo", "k_hi", "k_lo"))
    v_hi = m.sb("v_hi3", [TT, P], F32R)
    v_lo = m.sb("v_lo3", [TT, P], F32R)
    near = m.sb("near", [HEADS, NEAR])
    far = m.sb("bias_far", [HEADS])
    b_in = m.sb("b_in3", [3 * NA + 2 * NA])
    probs = m.sb("probs", [4, 2 * BLK])
    pT_hi = m.sb("pT_hi", [2, 2 * TPB, BLK], F32R)
    pT_lo = m.sb("pT_lo", [2, 2 * TPB, BLK], F32R)
    y_hi = m.sb("y_hi3", [2, BLK], F32R)
    y_lo = m.sb("y_lo3", [2, BLK], F32R)
    ident = m.sb("ident3", [P])
    mask_f = m.sb("mask_f32", [P + CHUNK])
    mask = m.sb("mask", [P + CHUNK], F32R)
    top_score, neg_max, total, inv_total = (m.sb(n, [4, 1]) for n in (
        "top_score", "neg_max", "total", "inv_total"))
    score = [m.ps(f"score{i}", 2 * BLK) for i in range(2)]
    turned_p = m.ps("probs_transposed", 2 * BLK)
    av = [m.ps(f"attended{i}", BLK) for i in range(2)]

    qkv_in = top.sem("qkv_in", NB)
    y_stored = top.sem("y_stored3", 2)
    (bias_in, consts_in, const, table_step, qk_done, top_step, neg_max_ready,
     exp_done, inv_ready, normed, turned, pT_hi_done, pT_lo_done, av_done, y_hi_done,
     y_lo_done) = (top.sem(n + "_3") for n in (
        "bias_in", "consts_in", "const", "table_step", "qk_done", "top_step",
        "neg_max_ready", "exp_done", "inv_ready", "normed", "turned", "pT_hi_done",
        "pT_lo_done", "av_done", "y_hi_done", "y_lo_done"))
    STEPS = NB * 2 * TPB
    GROUPS = NB * 2
    SLOTS = 4
    SCORE, NORM, TURN, SPLIT, ATTEND, OUT, DEPTH3 = 0, 1, 2, 3, 7, 11, 12

    def parts(s):
        return s // (2 * TPB), s // TPB % 2, s % TPB

    def columns(b, i):
        first = (i if b > 0 else TPB) * P
        return first, (i + TPB + 1) * P

    with nc.Block() as block:
        @block.sync
        def _(sp):
            for s, n in ((exp_done, CREDITS), (turned, SLOTS), (pT_lo_done, 1), (av_done, CREDITS),
                         (y_lo_done, CREDITS)):
                sp.sem_inc(s, n)
            for u in range(2):
                sp.sem_inc(y_stored[u], 16)

            def load(g, b):
                for name, dsts in (("q", (q_hi, q_lo)), ("k", (k_hi, k_lo))):
                    for part, dst in enumerate(dsts):
                        sp.dma_start(f32(dst[:, bass.ts(b, BLK)]),
                                     scr[name][part, bass.ds(g, 1), :, bass.ts(b, BLK)]
                                     .rearrange("k p t -> p (k t)")).then_inc(qkv_in[b], 16)
                for part, dst in enumerate((v_hi, v_lo)):
                    sp.dma_start(f32(dst[:, bass.ts(b, TPB), :]),
                                 scr["v"][part, bass.ts(b, BLK), bass.ds(g * P, P)]
                                 .rearrange("(j p) n -> p j n", p=P)).then_inc(qkv_in[b], 16)

            for b in range(NB):
                load(0, b)

            def body(g):
                last = isinstance(g, int)
                for b in range(NB):
                    whole(sp, top, (y_lo_done, GROUPS * g + 2 * b + 2 + CREDITS))
                    for part, src in ((0, y_hi), (1, y_lo)):
                        sp.dma_start(scr["yT"][part, bass.ds(g, 1), :, bass.ts(b, BLK)]
                                     .rearrange("k p t -> p (k t)"),
                                     f32(src[:, b % 2, :])).then_inc(y_stored[b % 2], 16)
                    if not last:
                        if b > 0:
                            load(g + 1, b - 1)
                        if b == NB - 1:
                            load(g + 1, b)

            rounds(sp, NA, body)
            for u in range(2):
                sp.wait_ge(y_stored[u], 16 + 32 * NA * NB // 2)

        @block.gpsimd
        def _(pool):
            identity(nc, pool, ident, const)
            nc.gpsimd.memset(mask_f[0:1, 0:CHUNK], 0.0).then_inc(const, 1)
            nc.gpsimd.memset(mask_f[0:1, CHUNK:P], NEG).then_inc(const, 1)
            nc.gpsimd.memset(mask_f[0:1, P:P + CHUNK], 1.0).then_inc(const, 1)

        @block.scalar
        def _(act):
            toeplitz = bass.AP(tensor=scr["bias_rows"].tensor, offset=P - 1,
                               ap=[[HEADS * BIAS_EXT - 1, P], [BIAS_EXT, HEADS], [1, NEAR]])
            act.dma_start(near[:, :, :], toeplitz).then_inc(bias_in, 16)
            act.dma_start(far[:, :], io["bias_far"].partition_broadcast(P)).then_inc(bias_in, 16)
            act.dma_start(b_in[:, :], io["b_in"]).then_inc(consts_in, 16)
            act.wait_ge(const, 5)
            nc.scalar.activation(mask[0:1, :], mask_f[0:1, :], ACT.Copy).then_inc(const, 1)
            act.wait_ge(consts_in, 16)

            def body(at):
                if step := at(SPLIT):
                    g, s = step
                    b, h, i = parts(s)
                    n = STEPS * g + s
                    lo, hi = columns(b, i)
                    u = s // TPB % 2
                    act.wait_ge(turned, n + 1 + SLOTS)
                    act.wait_ge(av_done, GROUPS * g + s // TPB + 1)
                    nc.scalar.activation(
                        pT_hi[:, u, lo // P:hi // P, bass.ts(i, P)],
                        turned_p[:, lo:hi].rearrange("p (j q) -> p j q", q=P), ACT.Copy
                    ).then_inc(pT_hi_done, 1)
                if step := at(SCORE):
                    g, s = step
                    b, h, i = parts(s)
                    n = STEPS * g + s
                    lo, hi = columns(b, i)
                    act.wait_ge(neg_max_ready, n + 1)
                    act.wait_ge(turned, n + 1)
                    nc.scalar.activation(probs[:, s % SLOTS, lo:hi], score[s % 2][:, lo:hi], ACT.Exp,
                                         scale=SCALE, bias=neg_max[:, s % SLOTS, :],
                                         accum_out=total[:, s % SLOTS, :]).then_inc(exp_done, 1)
                if (step := at(OUT)) and step[1] % TPB == 0:
                    g, s = step
                    b, h, _ = parts(s)
                    rows = slice(HD * h, HD * h + HD)
                    whole(act, top, (av_done, GROUPS * g + s // TPB + 1 + CREDITS),
                          (y_stored[b % 2], 16 + 32 * (NB // 2 * g + b // 2)))
                    nc.scalar.activation(y_hi[rows, b % 2, :], av[h][rows, :], ACT.Identity,
                                         bias=b_in[rows, bass.ds(g + 2 * NA, 1)]
                                         ).then_inc(y_hi_done, 1)

            sweep(act, NA, STEPS, DEPTH3, body)

        @block.vector
        def _(dve):
            dve.wait_ge(bias_in, 32)
            for h in range(HEADS):
                nc.vector.tensor_scalar(near[:, h, :], near[:, h, :], far[:, h:h + 1], 1.0 / SCALE,
                                        ALU.subtract, ALU.mult).then_inc(table_step, 1)
            dve.wait_ge(table_step, HEADS)
            nc.vector.memset(near[0:CHUNK, :, NEAR - CHUNK:NEAR], NEG).then_inc(table_step, 1)
            dve.wait_ge(table_step, HEADS + 1)
            dve.wait_ge(consts_in, 16)

            def body(at):
                if step := at(NORM):
                    g, s = step
                    b, h, i = parts(s)
                    n = STEPS * g + s
                    lo, hi = columns(b, i)
                    p = s % SLOTS
                    dve.wait_ge(exp_done, n + 1 + CREDITS)
                    nc.vector.reciprocal(inv_total[:, p, :], total[:, p, :]).then_inc(inv_ready, 1)
                    dve.wait_ge(inv_ready, n + 1)
                    nc.vector.tensor_scalar(probs[:, p, lo:hi], probs[:, p, lo:hi], inv_total[:, p, :],
                                            None, ALU.mult).then_inc(normed, 1)
                if step := at(SPLIT):
                    g, s = step
                    b, h, i = parts(s)
                    lo, hi = columns(b, i)
                    u = s // TPB % 2
                    dve.wait_ge(pT_hi_done, STEPS * g + s + 1)
                    nc.vector.tensor_tensor(
                        out=pT_lo[:, u, lo // P:hi // P, bass.ts(i, P)],
                        in0=turned_p[:, lo:hi].rearrange("p (j q) -> p j q", q=P),
                        in1=f32(pT_hi[:, u, lo // P:hi // P, bass.ts(i, P)]), op=ALU.subtract
                    ).then_inc(pT_lo_done, 1)
                if step := at(SCORE):
                    g, s = step
                    b, h, i = parts(s)
                    n = STEPS * g + s
                    lo, hi = columns(b, i)
                    p = s % SLOTS
                    sc = score[s % 2]
                    cut = max(lo, hi - NEAR)
                    dve.wait_ge(qk_done, n + 1)
                    nc.vector.tensor_tensor(
                        out=sc[:, cut:hi], in0=sc[:, cut:hi],
                        in1=near[:, bass.ds(2 * g + h, 1), NEAR - (hi - cut):NEAR]
                        .rearrange("p h c -> p (h c)"), op=ALU.add).then_inc(top_step, 1)
                    dve.wait_ge(top_step, 2 * n + 1)
                    nc.vector.tensor_reduce(top_score[:, p, :], sc[:, lo:hi], AX.X, ALU.max
                                            ).then_inc(top_step, 1)
                    dve.wait_ge(top_step, 2 * n + 2)
                    nc.vector.tensor_scalar(neg_max[:, p, :], top_score[:, p, :], -SCALE, None,
                                            ALU.mult).then_inc(neg_max_ready, 1)
                if (step := at(OUT)) and step[1] % TPB == 0:
                    g, s = step
                    b, h, _ = parts(s)
                    rows = slice(HD * h, HD * h + HD)
                    dve.wait_ge(y_hi_done, GROUPS * g + s // TPB + 1)
                    nc.vector.scalar_tensor_tensor(y_lo[rows, b % 2, :], av[h][rows, :],
                                                   b_in[rows, bass.ds(g + 2 * NA, 1)],
                                                   f32(y_hi[rows, b % 2, :]), ALU.add, ALU.subtract
                                                   ).then_inc(y_lo_done, 1)

            sweep(dve, NA, STEPS, DEPTH3, body)

        @block.tensor
        def _(pe):
            pe.wait_ge(const, 6)

            def body(at):
                if step := at(SCORE):
                    g, s = step
                    b, h, i = parts(s)
                    n = STEPS * g + s
                    sc = score[s % 2]
                    rows = slice(HD * h, HD * h + HD)
                    queries = slice(b * BLK + i * P, b * BLK + (i + 1) * P)
                    if s % (2 * TPB) == 0:
                        pe.wait_ge(qkv_in[b], 96 * g + 96)
                    pe.wait_ge(exp_done, n + 1)
                    if b > 0:
                        lo = i * P
                        keys = slice((b - 1) * BLK + i * P, b * BLK)
                        out = sc[:, lo:BLK]
                        nc.tensor.matmul(out, q_hi[rows, queries], k_hi[rows, keys], start=True, stop=False)
                        nc.tensor.matmul(sc[:, lo:lo + CHUNK], mask[0:1, 0:P], mask[0:1, P:P + CHUNK],
                                         start=False, stop=False)
                        nc.tensor.matmul(out, q_hi[rows, queries], k_lo[rows, keys], start=False, stop=False)
                        nc.tensor.matmul(out, q_lo[rows, queries], k_hi[rows, keys], start=False, stop=True)
                    keys = slice(b * BLK, b * BLK + (i + 1) * P)
                    three_passes(nc.tensor, sc[:, BLK:BLK + (i + 1) * P], q_hi[rows, queries],
                                 q_lo[rows, queries], k_hi[rows, keys], k_lo[rows, keys], True, True
                                 ).then_inc(qk_done, 1)
                if step := at(ATTEND):
                    g, s = step
                    b, h, part = parts(s)
                    group = GROUPS * g + s // TPB
                    order = [TPB + j for j in range(TPB)] + [j for j in range(TPB) if b > 0]
                    per = len(order) // TPB
                    if part == 0:
                        pe.wait_ge(pT_lo_done, STEPS * g + s + TPB + 1)
                        pe.wait_ge(y_lo_done, group + 1)
                    for n in range(part * per, (part + 1) * per):
                        j = order[n]
                        tile = b * TPB + j - TPB
                        cols = slice((j - TPB) * P, BLK) if j >= TPB else slice(0, (j + 1) * P)
                        last = three_passes(nc.tensor, av[h][:, cols], v_hi[:, tile, :], v_lo[:, tile, :],
                                            pT_hi[:, h, j, cols], pT_lo[:, h, j, cols],
                                            n == 0, n == len(order) - 1)
                    if part == TPB - 1:
                        last.then_inc(av_done, 1)
                if step := at(TURN):
                    g, s = step
                    b, h, i = parts(s)
                    n = STEPS * g + s
                    lo, hi = columns(b, i)
                    pe.wait_ge(normed, n + 1)
                    pe.wait_ge(pT_lo_done, n + 1)
                    for c in range(lo, hi, P):
                        last = nc.tensor.transpose(turned_p[:, c:c + P], probs[:, s % SLOTS, c:c + P],
                                                   ident[:, :])
                    last.then_inc(turned, 1)

            sweep(pe, NA, STEPS, DEPTH3, body)
    m.stack.close()


def phase4(nc, top, io, scr):
    m = top.phase()
    w_raw = m.sb("wo_raw", [2, D])
    w_hi = m.sb("wo_hi", [KD, D], F32R)
    w_lo = m.sb("wo_lo", [KD, D], F32R)
    y_hi = m.sb("y_hi", [2, KD, P], F32R)
    y_lo = m.sb("y_lo", [2, KD, P], F32R)
    h0 = m.sb("h0_tile", [2, D])
    res = m.sb("residual4", [2, D])
    h1 = m.sb("h1_tile", [2, D])
    h1T_hi = m.sb("h1T_hi", [2, KD, P], F32R)
    h1T_lo = m.sb("h1T_lo", [2, KD, P], F32R)
    bias = m.sb("b_out_row", [D])
    gain = m.sb("ln1_gain", [D])
    shift = m.sb("ln1_shift", [D])
    ident = m.sb("ident4", [P])
    stats = m.sb("stats4", [2, 12])
    mean_var = m.sb("mean_var4", [2, 2])
    var_eps = m.sb("var_eps4", [2, 1])
    minus_half = m.sb("minus_half4", [1])
    rstd = m.sb("rstd4", [2, 1])
    mix = [m.ps(f"mix{i}", D) for i in range(2)]
    tp = [m.ps(f"h1_transposed{i}", D) for i in range(2)]

    y_in, h0_in, h1_stored, h1T_stored, w_in = (top.sem(n, 2) for n in (
        "y_in4", "h0_in4", "h1_stored4", "h1T_stored4", "w_in4"))
    (rows_in, const, whi, wlo, mixed, summed, biased, stats_step, var_ready, rstd_ready,
     normed, gained, h1_ready, transposed, hhi_ready, hlo_ready) = (top.sem(n + "_4") for n in (
        "rows_in", "const", "whi", "wlo", "mixed", "summed", "biased", "stats_step",
        "var_ready", "rstd_ready", "normed", "gained", "h1_ready", "transposed", "hhi_ready",
        "hlo_ready"))
    DEPTH4 = 6
    LOAD, MIX, STATS, NORM, TURN, STORE = range(DEPTH4)

    with nc.Block() as block:
        @block.sync
        def _(sp):
            for s in (summed, normed, transposed, hlo_ready):
                sp.sem_inc(s, CREDITS)
            for u in range(2):
                sp.sem_inc(h1_stored[u], 16)
                sp.sem_inc(h1T_stored[u], 16)

            def body(at):
                if tile := at(LOAD):
                    j, u = tile
                    t = 2 * j + u
                    whole(sp, top, (summed, t + 1))
                    for part, dst in ((0, y_hi), (1, y_lo)):
                        sp.dma_start(f32(dst[:, u, :, :]),
                                     scr["yT"][part, :, :, bass.ts(t, P)].rearrange("k p t -> p k t")
                                     ).then_inc(y_in[u], 16)
                    sp.dma_start(h0[:, u, :], scr["h0"][bass.ts(t, P), :]).then_inc(h0_in[u], 16)
                if tile := at(NORM):
                    j, u = tile
                    t = 2 * j + u
                    whole(sp, top, (h1_ready, t + 1))
                    sp.dma_start(scr["h1"][bass.ts(t, P), :], h1[:, u, :]).then_inc(h1_stored[u], 16)
                if tile := at(STORE):
                    j, u = tile
                    t = 2 * j + u
                    whole(sp, top, (hlo_ready, t + 1 + CREDITS))
                    for part, src in ((0, h1T_hi), (1, h1T_lo)):
                        sp.dma_start(scr["h1T"][part, :, :, bass.ts(t, P)].rearrange("k p t -> p k t"),
                                     f32(src[:, u, :, :])).then_inc(h1T_stored[u], 16)

            ticks(sp, TT, DEPTH4, body)
            for u in range(2):
                sp.wait_ge(h1_stored[u], 16 + 16 * TT // 2)
                sp.wait_ge(h1T_stored[u], 16 + 32 * TT // 2)

        @block.gpsimd
        def _(pool):
            identity(nc, pool, ident, const)
            nc.gpsimd.memset(minus_half[:, :], -0.5).then_inc(const, 1)
            pool.wait_ge(const, 3)
            pool.wait_ge(rows_in, 48)

            def body(at):
                if tile := at(NORM):
                    j, u = tile
                    t = 2 * j + u
                    pool.wait_ge(gained, t + 1)
                    nc.gpsimd.tensor_tensor(out=h1[:, u, :], in0=h1[:, u, :], in1=shift[:, :],
                                            op=ALU.add).then_inc(h1_ready, 1)
                if tile := at(STATS):
                    j, u = tile
                    t = 2 * j + u
                    pool.wait_ge(var_ready, t + 1)
                    nc.gpsimd.tensor_tensor(out=rstd[:, u, :], in0=var_eps[:, u, :],
                                            in1=minus_half[:, :], op=ALU.pow).then_inc(rstd_ready, 1)
                if tile := at(MIX):
                    j, u = tile
                    t = 2 * j + u
                    pool.wait_ge(summed, t + 1 + CREDITS)
                    nc.gpsimd.tensor_tensor(out=res[:, u, :], in0=res[:, u, :], in1=bias[:, :],
                                            op=ALU.add).then_inc(biased, 1)

            ticks(pool, TT, DEPTH4, body)

        @block.scalar
        def _(act):
            for k in range(KD):
                if k >= 2:
                    act.wait_ge(wlo, k - 1)
                act.dma_start(w_raw[:, k % 2, :], io["w_out"][bass.ts(k, P), :]).then_inc(w_in[k % 2], 16)
                if k == 1:
                    for dst, name in ((bias, "b_out"), (gain, "ln1_g"), (shift, "ln1_b")):
                        act.dma_start(dst[:, :], io[name].partition_broadcast(P)).then_inc(rows_in, 16)
                if k >= 1:
                    act.wait_ge(w_in[(k - 1) % 2], 16 * ((k - 1) // 2 + 1))
                    nc.scalar.activation(w_hi[:, k - 1, :], w_raw[:, (k - 1) % 2, :], ACT.Copy
                                         ).then_inc(whi, 1)
            act.wait_ge(w_in[(KD - 1) % 2], 16 * KD // 2)
            nc.scalar.activation(w_hi[:, KD - 1, :], w_raw[:, (KD - 1) % 2, :], ACT.Copy).then_inc(whi, 1)

            def body(at):
                if tile := at(TURN):
                    j, u = tile
                    t = 2 * j + u
                    act.wait_ge(transposed, t + 1 + CREDITS)
                    act.wait_ge(h1T_stored[u], 16 + 32 * j)
                    nc.scalar.activation(h1T_hi[:, u, :, :].rearrange("p k t -> p (k t)"), tp[u][:, :],
                                         ACT.Copy).then_inc(hhi_ready, 1)

            ticks(act, TT, DEPTH4, body)

        @block.vector
        def _(dve):
            for k in range(KD):
                dve.wait_ge(whi, k + 1)
                nc.vector.tensor_tensor(out=w_lo[:, k, :], in0=w_raw[:, k % 2, :], in1=f32(w_hi[:, k, :]),
                                        op=ALU.subtract).then_inc(wlo, 1)
            dve.wait_ge(rows_in, 48)

            def body(at):
                if tile := at(TURN):
                    j, u = tile
                    t = 2 * j + u
                    dve.wait_ge(hhi_ready, t + 1)
                    nc.vector.tensor_tensor(out=h1T_lo[:, u, :, :].rearrange("p k t -> p (k t)"),
                                            in0=tp[u][:, :],
                                            in1=f32(h1T_hi[:, u, :, :]).rearrange("p k t -> p (k t)"),
                                            op=ALU.subtract).then_inc(hlo_ready, 1)
                if tile := at(NORM):
                    j, u = tile
                    t = 2 * j + u
                    dve.wait_ge(rstd_ready, t + 1)
                    dve.wait_ge(transposed, t + 1)
                    dve.wait_ge(h1_stored[u], 16 * (j + 1))
                    nc.vector.tensor_scalar(h1[:, u, :], res[:, u, :], mean_var[:, u, 0:1],
                                            rstd[:, u, :], ALU.subtract, ALU.mult).then_inc(normed, 1)
                    dve.wait_ge(normed, t + 1 + CREDITS)
                    nc.vector.tensor_tensor(out=h1[:, u, :], in0=h1[:, u, :], in1=gain[:, :],
                                            op=ALU.mult).then_inc(gained, 1)
                if tile := at(STATS):
                    j, u = tile
                    t = 2 * j + u
                    dve.wait_ge(biased, t + 1)
                    nc.vector.bn_stats(stats[:, u, 0:6], res[:, u, 0:D // 2])
                    nc.vector.bn_stats(stats[:, u, 6:12], res[:, u, D // 2:D]).then_inc(stats_step, 1)
                    whole(dve, top, (stats_step, 2 * t + 1))
                    nc.vector.bn_aggr(mean_var[:, u, :], stats[:, u, :]).then_inc(stats_step, 1)
                    dve.wait_ge(stats_step, 2 * t + 2)
                    nc.vector.tensor_scalar(var_eps[:, u, :], mean_var[:, u, 1:2], EPS, None,
                                            ALU.add).then_inc(var_ready, 1)
                if tile := at(MIX):
                    j, u = tile
                    t = 2 * j + u
                    dve.wait_ge(mixed, t + 1)
                    dve.wait_ge(h0_in[u], 16 * (j + 1))
                    dve.wait_ge(normed, t + 1)
                    nc.vector.scalar_tensor_tensor(res[:, u, :], h0[:, u, :], ALPHA, mix[u][:, :],
                                                   ALU.mult, ALU.add).then_inc(summed, 1)

            ticks(dve, TT, DEPTH4, body)

        @block.tensor
        def _(pe):
            pe.wait_ge(const, 2)

            def body(at):
                if tile := at(TURN):
                    j, u = tile
                    t = 2 * j + u
                    pe.wait_ge(h1_ready, t + 1)
                    pe.wait_ge(hlo_ready, t + 1)
                    for k in range(KD):
                        last = nc.tensor.transpose(tp[u][:, bass.ts(k, P)], h1[:, u, bass.ts(k, P)],
                                                   ident[:, :])
                    last.then_inc(transposed, 1)
                if tile := at(MIX):
                    j, u = tile
                    t = 2 * j + u
                    first = isinstance(t, int) and t == 0
                    pe.wait_ge(y_in[u], 32 * (j + 1))
                    pe.wait_ge(summed, t + 1)
                    for k in range(KD):
                        if first:
                            pe.wait_ge(wlo, k + 1)
                        last = token_major(nc.tensor, mix[u], y_hi[:, u, k, :], y_lo[:, u, k, :],
                                           w_hi[:, k, :], w_lo[:, k, :], k == 0, k == KD - 1)
                    last.then_inc(mixed, 1)

            ticks(pe, TT, DEPTH4, body)
    m.stack.close()


def phase5(nc, top, io, scr):
    m = top.phase()
    hT_hi = m.sb("hT_hi5", [KD, T], F32R)
    hT_lo = m.sb("hT_lo5", [KD, T], F32R)
    w_raw = m.sb("w_raw5", [2, KD, P])
    w_hi = m.sb("w_hi5", [2, KD, P], F32R)
    w_lo = m.sb("w_lo5", [2, KD, P], F32R)
    up = [m.sb(f"up_{n}", [FW - 1 + T]) for n in ("value", "gate")]
    value = m.sb("conv_value", [T])
    gate = m.sb("conv_gate", [2, BLK])
    vecs = m.sb("ffn_vectors", [FW + 2, 2 * NF])
    TAP, CONV_B, B_UP = 0, FW, FW + 1
    mm = [m.ps(f"mm5_{i}", BLK) for i in range(2)]

    hT_in = top.sem("hT_in5", NB)
    w_in, hidden_stored = (top.sem(n, 2) for n in ("w_in5", "hidden_stored5"))
    (consts_in, pad_ready, whi, w_split, mm_ready, evac, conv_step, value_done, gate_done, gelu_done,
     hidden_ready) = (top.sem(n + "_5") for n in (
        "consts_in", "pad_ready", "whi", "w_split", "mm_ready", "evac", "conv_step", "value_done",
        "gate_done", "gelu_done", "hidden_ready"))
    VALUE, GATE = range(2)
    GROUPS = 2 * NB
    MM0 = 2 * NB

    with nc.Block() as block:
        @block.sync
        def _(sp):
            for s, n in ((w_split, CREDITS), (evac, CREDITS), (mm_ready, MM0), (value_done, 1),
                         (gate_done, 1), (hidden_ready, CREDITS)):
                sp.sem_inc(s, n)
            for u in range(2):
                sp.sem_inc(hidden_stored[u], 16)

            def load(t, c):
                whole(sp, top, (w_split, 2 * t + c + 1))
                cols = io["ffn_w_up"][:, bass.ds(t * P + c * FF, P)]
                sp.dma_start(w_raw[:, c, :, :], cols.rearrange("(k p) n -> p k n", p=P)
                             ).then_inc(w_in[c], 16)

            load(0, VALUE)
            for b in range(NB):
                for part, dst in ((0, hT_hi), (1, hT_lo)):
                    sp.dma_start(f32(dst[:, :, bass.ts(b, BLK)]),
                                 scr["h1T"][part, :, :, bass.ts(b, BLK)].rearrange("k p t -> p k t")
                                 ).then_inc(hT_in[b], 16)
                if b == 0:
                    load(0, GATE)

            def body(t):
                last = isinstance(t, int)
                for c in range(2):
                    if not last:
                        load(t + 1, c)
                    for b in range(NB):
                        if c == GATE:
                            whole(sp, top, (hidden_ready, NB * t + b + 1 + CREDITS))
                            sp.dma_start(scr["hidden"][bass.ds(t, 1), :, bass.ts(b, BLK)]
                                         .rearrange("k p t -> p (k t)"), gate[:, b % 2, :]
                                         ).then_inc(hidden_stored[b % 2], 16)

            rounds(sp, NF, body)
            for u in range(2):
                sp.wait_ge(hidden_stored[u], 16 + 16 * NB * NF // 2)

        @block.gpsimd
        def _(pool):
            for buf in up:
                nc.gpsimd.memset(buf[:, 0:FW - 1], 0.0).then_inc(pad_ready, 1)

        @block.scalar
        def _(act):
            act.dma_start(vecs[:, :, :], io["ffn_vectors"]).then_inc(consts_in, 16)

            def hi(t, c):
                act.wait_ge(w_in[c], 16 * t + 16)
                act.wait_ge(mm_ready, GROUPS * t + NB * c - NB + MM0)
                nc.scalar.activation(w_hi[:, c, :, :].rearrange("p k n -> p (k n)"),
                                     w_raw[:, c, :, :].rearrange("p k n -> p (k n)"),
                                     ACT.Copy).then_inc(whi, 1)

            hi(0, VALUE)
            act.wait_ge(consts_in, 16)

            def body(t):
                last = isinstance(t, int)
                for c in range(2):
                    for b in range(NB):
                        whole(act, top, (mm_ready, GROUPS * t + NB * c + b + 1 + MM0),
                              ((value_done, gate_done)[c], NB * t + 1))
                        nc.scalar.activation(up[c][:, bass.ds(FW - 1 + b * BLK, BLK)], mm[b % 2][:, :],
                                             ACT.Identity, bias=vecs[:, B_UP, bass.ds(t + c * NF, 1)]
                                             ).then_inc(evac, 1)
                        if b == 0 and not (last and c == GATE):
                            hi(t + c, 1 - c)
                        if c == GATE:
                            act.wait_ge(gate_done, NB * t + b + 2)
                            nc.scalar.activation(gate[:, b % 2, :], gate[:, b % 2, :],
                                                 ACT.Gelu_apprx_tanh).then_inc(gelu_done, 1)

            rounds(act, NF, body)

        @block.vector
        def _(dve):
            def lo(t, c):
                dve.wait_ge(whi, 2 * t + c + 1)
                nc.vector.tensor_tensor(out=w_lo[:, c, :, :].rearrange("p k n -> p (k n)"),
                                        in0=w_raw[:, c, :, :].rearrange("p k n -> p (k n)"),
                                        in1=f32(w_hi[:, c, :, :]).rearrange("p k n -> p (k n)"),
                                        op=ALU.subtract).then_inc(w_split, 1)

            lo(0, VALUE)
            dve.wait_ge(pad_ready, 2)

            def body(t):
                last = isinstance(t, int)
                for c in range(2):
                    vec = lambda row: vecs[:, row, bass.ds(t + c * NF, 1)]
                    for b in range(NB):
                        n = GROUPS * t + NB * c + b
                        dve.wait_ge(evac, n + 1 + CREDITS)
                        if c == VALUE:
                            dve.wait_ge(hidden_ready, NB * t + CREDITS)
                            out, done = value[:, bass.ts(b, BLK)], value_done
                        else:
                            dve.wait_ge(hidden_stored[b % 2], 16 + 16 * (2 * t + b // 2))
                            out, done = gate[:, b % 2, :], gate_done
                        nc.vector.tensor_scalar(out, up[c][:, bass.ds(b * BLK, BLK)], vec(TAP),
                                                vec(CONV_B), ALU.mult, ALU.add).then_inc(conv_step, 1)
                        for k in range(1, FW):
                            dve.wait_ge(conv_step, (FW - 1) * n + k)
                            nc.vector.scalar_tensor_tensor(
                                out, up[c][:, bass.ds(b * BLK + k, BLK)], vec(TAP + k), out,
                                ALU.mult, ALU.add).then_inc(conv_step if k < FW - 1 else done, 1)
                        if b == 0 and not (last and c == GATE):
                            lo(t + c, 1 - c)
                        if c == GATE:
                            dve.wait_ge(gelu_done, NB * t + b + 1)
                            nc.vector.tensor_tensor(out=gate[:, b % 2, :], in0=gate[:, b % 2, :],
                                                    in1=value[:, bass.ts(b, BLK)], op=ALU.mult
                                                    ).then_inc(hidden_ready, 1)

            rounds(dve, NF, body)

        @block.tensor
        def _(pe):
            def body(t):
                for c in range(2):
                    pe.wait_ge(w_split, 2 * t + c + 1 + CREDITS)
                    for b in range(NB):
                        if c == VALUE:
                            pe.wait_ge(hT_in[b], 32)
                        pe.wait_ge(evac, GROUPS * t + NB * c + b + 1)
                        for k in range(KD):
                            done = three_passes(nc.tensor, mm[b % 2][:, :], w_hi[:, c, k, :],
                                                w_lo[:, c, k, :], hT_hi[:, k, bass.ts(b, BLK)],
                                                hT_lo[:, k, bass.ts(b, BLK)], k == 0, k == KD - 1)
                        done.then_inc(mm_ready, 1)

            rounds(pe, NF, body)
    m.stack.close()


def phase6(nc, top, io, scr, out):
    m = top.phase()
    w_raw = m.sb("wd_raw", [2, D])
    w_hi = m.sb("wd_hi", [2, D], F32R)
    w_lo = m.sb("wd_lo", [2, D], F32R)
    g_raw = m.sb("hidden_raw", [2, BLK])
    g_hi = m.sb("hidden_hi", [2, BLK], F32R)
    g_lo = m.sb("hidden_lo", [2, BLK], F32R)
    h1 = m.sb("h1_block", [TPB, D])
    res = m.sb("residual6", [TPB, D])
    y = m.sb("out_block", [TPB, D])
    bias = m.sb("b_down_row", [D])
    gain = m.sb("ln2_gain", [D])
    shift = m.sb("ln2_shift", [D])
    stats = m.sb("stats6", [TPB, 12])
    mean_var = m.sb("mean_var6", [TPB, 2])
    var_eps = m.sb("var_eps6", [TPB, 1])
    minus_half = m.sb("minus_half6", [1])
    rstd = m.sb("rstd6", [TPB, 1])
    acc = [m.ps(f"down{i}", D) for i in range(TPB)]

    raw_in = top.sem("raw_in6", 2)
    out_stored = top.sem("out_stored6", TPB)
    (rows_in, const, h1_in, hi_ready, split, used, tile_done, summed, biased, stats_step,
     var_ready, rstd_ready, normed, gained, out_ready) = (top.sem(n + "_6") for n in (
        "rows_in", "const", "h1_in", "hi_ready", "split", "used", "tile_done", "summed", "biased",
        "stats_step", "var_ready", "rstd_ready", "normed", "gained", "out_ready"))
    HEAD = 6

    def run(engine_round, step, beside, evacuate):
        for k in range(HEAD):
            step(0, k)

        def body(t):
            last = isinstance(t, int)
            for k in range(HEAD, NF):
                step(t, k)
            evacuate(t)
            for k in range(HEAD):
                if not last:
                    step(t + 1, k)
                beside(t, k)

        rounds(engine_round, NB, body)

    with nc.Block() as block:
        @block.sync
        def _(sp):
            for s, n in ((split, CREDITS), (used, CREDITS), (summed, TPB), (normed, TPB)):
                sp.sem_inc(s, n)
            for i in range(TPB):
                sp.sem_inc(out_stored[i], 16)

            def load(t, k):
                whole(sp, top, (split, NF * t + k + 1))
                sp.dma_start(w_raw[:, k % 2, :], io["ffn_w_down"][bass.ts(k, P), :]
                             ).then_inc(raw_in[k % 2], 16)
                sp.dma_start(g_raw[:, k % 2, :], scr["hidden"][k, :, bass.ts(t, BLK)]
                             ).then_inc(raw_in[k % 2], 16)

            def load_residual(t):
                whole(sp, top, (summed, TPB * t + TPB))
                sp.dma_start(h1[:, :, :], scr["h1"][bass.ts(t, BLK), :]
                             .rearrange("(i p) d -> p i d", p=P)).then_inc(h1_in, 16)

            def step(t, k):
                load(t, k)
                if k == HEAD:
                    load_residual(t)

            def beside(t, k):
                if k >= HEAD - TPB:
                    i = k - (HEAD - TPB)
                    whole(sp, top, (out_ready, TPB * t + i + 1))
                    sp.dma_start(out[bass.ds(t * BLK + i * P, P), :], y[:, i, :]
                                 ).then_inc(out_stored[i], 16)

            run(sp, step, beside, lambda t: None)
            for i in range(TPB):
                sp.wait_ge(out_stored[i], 16 + 16 * NB)

        @block.gpsimd
        def _(pool):
            nc.gpsimd.memset(minus_half[:, :], -0.5).then_inc(const, 1)
            pool.wait_ge(const, 1)
            pool.wait_ge(rows_in, 48)

            def add_bias(t, i):
                pool.wait_ge(summed, TPB * t + i + 1 + TPB)
                nc.gpsimd.tensor_tensor(out=res[:, i, :], in0=res[:, i, :], in1=bias[:, :],
                                        op=ALU.add).then_inc(biased, 1)

            def power(t, i):
                pool.wait_ge(var_ready, TPB * t + i + 1)
                nc.gpsimd.tensor_tensor(out=rstd[:, i, :], in0=var_eps[:, i, :],
                                        in1=minus_half[:, :], op=ALU.pow).then_inc(rstd_ready, 1)

            def add_shift(t, i):
                pool.wait_ge(gained, TPB * t + i + 1)
                nc.gpsimd.tensor_tensor(out=y[:, i, :], in0=y[:, i, :], in1=shift[:, :],
                                        op=ALU.add).then_inc(out_ready, 1)

            def beside(t, k):
                if k < TPB:
                    add_bias(t, k)
                if 1 <= k <= TPB:
                    power(t, k - 1)
                if k >= 2:
                    add_shift(t, k - 2)

            run(pool, lambda t, k: None, beside, lambda t: None)

        @block.scalar
        def _(act):
            for dst, name in ((bias, "ffn_b_down"), (gain, "ln2_g"), (shift, "ln2_b")):
                act.dma_start(dst[:, :], io[name].partition_broadcast(P)).then_inc(rows_in, 16)

            def step(t, k):
                act.wait_ge(raw_in[k % 2], 32 * (NF // 2 * t + k // 2 + 1))
                act.wait_ge(used, NF * t + k + 1)
                nc.scalar.activation(w_hi[:, k % 2, :], w_raw[:, k % 2, :], ACT.Copy)
                nc.scalar.activation(g_hi[:, k % 2, :], g_raw[:, k % 2, :], ACT.Copy
                                     ).then_inc(hi_ready, 1)

            run(act, step, lambda t, k: None, lambda t: None)

        @block.vector
        def _(dve):
            dve.wait_ge(rows_in, 48)

            def step(t, k):
                dve.wait_ge(hi_ready, NF * t + k + 1)
                nc.vector.tensor_tensor(out=w_lo[:, k % 2, :], in0=w_raw[:, k % 2, :],
                                        in1=f32(w_hi[:, k % 2, :]), op=ALU.subtract)
                nc.vector.tensor_tensor(out=g_lo[:, k % 2, :], in0=g_raw[:, k % 2, :],
                                        in1=f32(g_hi[:, k % 2, :]), op=ALU.subtract
                                        ).then_inc(split, 1)

            def evacuate(t):
                for i in range(TPB):
                    if i == 0:
                        dve.wait_ge(h1_in, 16 * t + 16)
                        dve.wait_ge(normed, TPB * t + TPB)
                    if i < TPB - 1:
                        dve.wait_ge(tile_done, (TPB - 1) * t + i + 1)
                    else:
                        dve.wait_ge(used, NF * t + NF + CREDITS)
                    nc.vector.scalar_tensor_tensor(res[:, i, :], h1[:, i, :], ALPHA, acc[i][:, :],
                                                   ALU.mult, ALU.add).then_inc(summed, 1)

            def beside(t, k):
                if 1 <= k <= TPB:
                    i = k - 1
                    n = TPB * t + i
                    dve.wait_ge(biased, n + 1)
                    nc.vector.bn_stats(stats[:, i, 0:6], res[:, i, 0:D // 2])
                    nc.vector.bn_stats(stats[:, i, 6:12], res[:, i, D // 2:D]).then_inc(stats_step, 1)
                    whole(dve, top, (stats_step, 2 * n + 1))
                    nc.vector.bn_aggr(mean_var[:, i, :], stats[:, i, :]).then_inc(stats_step, 1)
                    dve.wait_ge(stats_step, 2 * n + 2)
                    nc.vector.tensor_scalar(var_eps[:, i, :], mean_var[:, i, 1:2], EPS, None,
                                            ALU.add).then_inc(var_ready, 1)
                if k >= 2:
                    i = k - 2
                    n = TPB * t + i
                    dve.wait_ge(rstd_ready, n + 1)
                    dve.wait_ge(out_stored[i], 16 * t + 16)
                    nc.vector.tensor_scalar(y[:, i, :], res[:, i, :], mean_var[:, i, 0:1],
                                            rstd[:, i, :], ALU.subtract, ALU.mult).then_inc(normed, 1)
                    dve.wait_ge(normed, n + 1 + TPB)
                    nc.vector.tensor_tensor(out=y[:, i, :], in0=y[:, i, :], in1=gain[:, :],
                                            op=ALU.mult).then_inc(gained, 1)

            run(dve, step, beside, evacuate)

        @block.tensor
        def _(pe):
            def step(t, k):
                pe.wait_ge(split, NF * t + k + 1 + CREDITS)
                for i in range(TPB):
                    if k == 0:
                        pe.wait_ge(summed, TPB * t + i + 1)
                    done = token_major(nc.tensor, acc[i], g_hi[:, k % 2, bass.ts(i, P)],
                                       g_lo[:, k % 2, bass.ts(i, P)], w_hi[:, k % 2, :],
                                       w_lo[:, k % 2, :], k == 0, k == NF - 1)
                    if i == TPB - 1:
                        done.then_inc(used, 1)
                    elif k == NF - 1:
                        done.then_inc(tile_done, 1)

            run(pe, step, lambda t, k: None, lambda t: None)
    m.stack.close()


def program(nc, io, out, scratch, phases=(1, 2, 3, 4, 5, 6)):
    scr = {name: scratch(name, shape) for name, shape in (
        ("h0", [T, D]), ("h0T", [2, KD, P, T]), ("v", [2, T, DA]), ("q", [2, NA, P, T]),
        ("k", [2, NA, P, T]), ("yT", [2, KD, P, T]), ("h1", [T, D]), ("h1T", [2, KD, P, T]),
        ("hidden", [NF, P, T]), ("bias_ext", [HEADS, BIAS_EXT]),
        ("bias_rows", [P, HEADS, BIAS_EXT]))}
    with ExitStack() as stack:
        top = Tools(nc, stack)
        top.started = top.sem("started")
        with nc.Block() as block:
            @block.sync
            def _(sp):
                sp.sem_inc(top.started, 1)

        for n, f in ((1, phase1), (2, phase2), (3, phase3), (4, phase4), (5, phase5)):
            if n in phases:
                f(nc, top, io, scr)
        if 6 in phases:
            phase6(nc, top, io, scr, out)


def host_layout(inputs):
    a = {k: np.ascontiguousarray(v) for k, v in inputs.items()}
    out = {n: a[n].reshape(a[n].shape[1:]) for n in a if n not in ("ln_in_g", "ln_in_b")}
    out["ln_in_g"], out["ln_in_b"] = a["ln_in_g"], a["ln_in_b"]
    by_tile = lambda v: np.ascontiguousarray(v.reshape(-1, P).T)
    lru = [a["lru_conv_w"][0, k] for k in range(CW)]
    lru += [a[n][0] for n in ("lru_conv_b", "lru_b_a", "lru_b_x", "lru_lambda")]
    out["lru_vectors"] = np.ascontiguousarray(np.stack([by_tile(v) for v in lru], axis=1))
    out["b_in"] = by_tile(a["b_in"][0])
    ffn = [a["ffn_conv_w"][0, k] for k in range(FW)] + [a["ffn_conv_b"][0], a["ffn_b_up"][0]]
    out["ffn_vectors"] = np.ascontiguousarray(np.stack([by_tile(v) for v in ffn], axis=1))
    gate_w = np.zeros((NA, P, 2, P), np.float32)
    for g, name in enumerate(("lru_w_a", "lru_w_x")):
        for n, w in enumerate(a[name][0]):
            s = slice(HD * (n % 2), HD * (n % 2) + HD)
            gate_w[n // 2, s, g, s] = w
    out["gate_w"] = gate_w
    out["rel_bias_reversed"] = np.ascontiguousarray(a["rel_bias"][0, :, ::-1])
    out["bias_far"] = np.ascontiguousarray(a["rel_bias"][0, :, -1])
    for n in ("rel_bias", "lru_conv_w", "lru_conv_b", "lru_b_a", "lru_b_x", "lru_lambda", "lru_w_a",
              "lru_w_x", "ffn_conv_w", "ffn_conv_b", "ffn_b_up"):
        del out[n]
    return out


def kernel(**inputs):
    import concourse.bacc as bacc
    from concourse.bass_utils import run_bass_kernel_spmd as run

    nc = bacc.Bacc("TRN2", target_bir_lowering=False, num_devices=1)
    arrays = {f"in_{name}": a for name, a in host_layout(inputs).items()}
    io = {name[3:]: nc.dram_tensor(name, a.shape, F32, kind="ExternalInput").ap()
          for name, a in arrays.items()}
    out = nc.dram_tensor("out", [T, D], F32, kind="ExternalOutput").ap()

    def scratch(name, shape):
        return nc.dram_tensor(f"scratch_{name}", shape, F32, kind="Internal").ap()

    program(nc, io, out, scratch)
    result = run(nc, [arrays], core_ids=[0])
    return result.results[0]["out"].reshape(inputs["x"].shape)
```

```python
from contextlib import ExitStack

import numpy as np

import concourse.bass as bass
from concourse import mybir

F32 = mybir.dt.float32
F32R = mybir.dt.float32r
ALU = mybir.AluOpType
ACT = mybir.ActivationFunctionType
AX = mybir.AxisListType

P = 128
T, D = 2048, 1024
KD = D // P
DA = 512
NA = DA // P
HEADS, HD = 8, 64
CHUNK, LEFT, MAX_REL = 64, 8, 128
N_REL = CHUNK - 1 + MAX_REL + 1
FF = 2816
NF = FF // P
TT = T // P
BLK = 512
NB = T // BLK
TPB = BLK // P
EPS = 1e-5
ALPHA = 2.0 ** 0.25
SCALE = HD ** -0.5
NEG = -1e30
LRU_C = 8.0
CW, FW = 4, 3
CREDITS = 2
NEAR = 2 * P
BIAS_EXT = NEAR + P - 1
assert LEFT * CHUNK == BLK and NEAR - P >= MAX_REL


def ticks(eng, count, depth, body):
    first = depth + depth % 2
    last = count - count % 2

    def fixed(n):
        return lambda k: divmod(n - k, 2) if 0 <= n - k < count else None

    for n in range(first):
        body(fixed(n))
    with eng.Fori(first // 2, last // 2) as g:
        for u in range(2):
            body(lambda k, u=u: (g + (u - k) // 2, (u - k) % 2))
    for n in range(last, count + depth - 1):
        body(fixed(n))


def whole(eng, top, *waits):
    for _, value in waits:
        if not isinstance(value, int):
            eng.compute_val(value)
    eng.wait_ge(top.started, 1)
    for sem, value in waits:
        eng.wait_ge(sem, value)


def rounds(eng, count, body):
    with eng.Fori(0, count - 1) as t:
        body(t)
    body(count - 1)


def three_passes(pe, out, w_hi, w_lo, x_hi, x_lo, start, stop):
    pe.matmul(out, w_hi, x_hi, start=start, stop=False)
    pe.matmul(out, w_hi, x_lo, start=False, stop=False)
    return pe.matmul(out, w_lo, x_hi, start=False, stop=stop)


def token_major(pe, out, x_hi, x_lo, w_hi, w_lo, start, stop):
    halves = [slice(0, BLK), slice(BLK, D)]
    for x, w, first in ((x_hi, w_hi, start), (x_hi, w_lo, False), (x_lo, w_hi, False)):
        for half in halves:
            last = pe.matmul(out[:, half], x, w[:, half], start=first, stop=stop and x is x_lo)
    return last


class Tools:

    def __init__(self, nc, stack):
        self.nc, self.stack = nc, stack

    def sem(self, name, n=None):
        one = lambda x: self.stack.enter_context(self.nc.semaphore(x))
        return one(name) if n is None else [one(f"{name}_{i}") for i in range(n)]

    def phase(self):
        return Tools(self.nc, ExitStack())

    def sb(self, name, shape, dt=F32):
        return self.stack.enter_context(self.nc.sbuf_tensor(name, [P, *shape], dt))

    def ps(self, name, cols):
        return self.stack.enter_context(self.nc.psum_tensor(name, [P, cols], F32))


def f32(x):
    return x.bitcast(F32)


def identity(nc, pool, ident, sem):
    nc.gpsimd.memset(ident[:, :], 0.0).then_inc(sem, 1)
    pool.wait_ge(sem, 1)
    nc.gpsimd.affine_select(out=ident[:, :], in_=ident[:, :], compare_op=ALU.not_equal, fill=1.0,
                            base=0, pattern=[[-1, P]], channel_multiplier=1).then_inc(sem, 1)


def phase1(nc, top, io, scr, hT_hi, hT_lo, w_raw, load_next):
    m = top.phase()
    x_sb = m.sb("x_sb", [2, D])
    h_sb = m.sb("h_sb", [2, D])
    wv_hi = m.sb("wv_hi", [KD, DA], F32R)
    wv_lo = m.sb("wv_lo", [KD, DA], F32R)
    v_hi = m.sb("v_hi", [2, DA], F32R)
    v_lo = m.sb("v_lo", [2, DA], F32R)
    gain = m.sb("ln_in_gain", [D])
    shift = m.sb("ln_in_shift", [D])
    ident = m.sb("ident1", [P])
    stats = m.sb("stats1", [2, 12])
    mean_var = m.sb("mean_var1", [2, 2])
    var_eps = m.sb("var_eps1", [2, 1])
    minus_half = m.sb("minus_half1", [1])
    rstd = m.sb("rstd1", [2, 1])
    tp = [m.ps(f"h_transposed{i}", D) for i in range(2)]
    vp = [m.ps(f"v_psum{i}", DA) for i in range(2)]

    x_loaded, h_stored, v_stored = (top.sem(n, 2) for n in ("x_loaded", "h_stored", "v_stored"))
    WV_SLOTS = 4
    wv_loaded = top.sem("wv_loaded", WV_SLOTS)
    (rows_loaded, const1, stats_step, var_ready, rstd_ready, normed, gained,
     h_ready, transposed, hhi_ready, hlo_ready, wvhi_ready, wvlo_ready, v_ready, vhi_ready,
     vlo_ready) = map(top.sem, (
        "rows_loaded", "const1", "stats_step", "var_ready", "rstd_ready",
        "normed", "gained", "h_ready", "transposed", "hhi_ready", "hlo_ready", "wvhi_ready",
        "wvlo_ready", "v_ready", "vhi_ready", "vlo_ready"))
    bias_stored, rel_in, ext_ready = (top.sem(n) for n in ("bias_stored", "rel_in", "ext_ready"))
    ext_sb = m.sb("bias_ext_sb", [BIAS_EXT])
    DEPTH1 = 6
    LOAD, STATS, NORM, TURN, VALUE, STORE_V = range(DEPTH1)

    def wv_raw(k):
        flat = w_raw[:, :, :, :].rearrange("p s k n -> p (s k n)")
        return flat[:, bass.ts(k % WV_SLOTS, DA)]

    with nc.Block() as block:
        @block.sync
        def _(sp):
            for s in (normed, transposed, hlo_ready, vlo_ready):
                sp.sem_inc(s, CREDITS)
            for u in range(2):
                for s in (h_stored, v_stored):
                    sp.sem_inc(s[u], 16)
            def body(at):
                if tile := at(STORE_V):
                    j, u = tile
                    t = 2 * j + u
                    whole(sp, top, (vlo_ready, t + 1 + CREDITS))
                    for part, src in ((0, v_hi), (1, v_lo)):
                        sp.dma_start(scr["v"][part, bass.ts(t, P), :],
                                     f32(src[:, u, :])).then_inc(v_stored[u], 16)
                if tile := at(LOAD):
                    j, u = tile
                    t = 2 * j + u
                    whole(sp, top, (normed, t + 1))
                    sp.dma_start(x_sb[:, u, :], io["x"][bass.ts(t, P), :]).then_inc(x_loaded[u], 16)
                if tile := at(TURN):
                    j, u = tile
                    t = 2 * j + u
                    whole(sp, top, (h_ready, t + 1))
                    sp.dma_start(scr["h0"][bass.ts(t, P), :], h_sb[:, u, :]).then_inc(h_stored[u], 16)

            ticks(sp, TT, DEPTH1, body)
            sp.wait_ge(wvlo_ready, KD)
            load_next(sp)
            for u in range(2):
                sp.wait_ge(h_stored[u], 16 + 16 * TT // 2)
                sp.wait_ge(v_stored[u], 16 + 32 * TT // 2)
            sp.wait_ge(bias_stored, 32)

        @block.gpsimd
        def _(pool):
            identity(nc, pool, ident, const1)
            nc.gpsimd.memset(minus_half[:, :], -0.5).then_inc(const1, 1)
            pool.wait_ge(const1, 3)
            pool.wait_ge(rows_loaded, 32)

            def body(at):
                if tile := at(NORM):
                    j, u = tile
                    t = 2 * j + u
                    pool.wait_ge(gained, t + 1)
                    nc.gpsimd.tensor_tensor(out=h_sb[:, u, :], in0=h_sb[:, u, :], in1=shift[:, :],
                                            op=ALU.add).then_inc(h_ready, 1)
                if tile := at(STATS):
                    j, u = tile
                    t = 2 * j + u
                    pool.wait_ge(var_ready, t + 1)
                    pool.wait_ge(normed, t + 1)
                    nc.gpsimd.tensor_tensor(out=rstd[:, u, :], in0=var_eps[:, u, :],
                                            in1=minus_half[:, :], op=ALU.pow).then_inc(rstd_ready, 1)

            ticks(pool, TT, DEPTH1, body)

        @block.scalar
        def _(act):
            act.dma_start(gain[:, :], io["ln_in_g"].partition_broadcast(P)).then_inc(rows_loaded, 16)
            act.dma_start(shift[:, :], io["ln_in_b"].partition_broadcast(P)).then_inc(rows_loaded, 16)
            act.wait_ge(ext_ready, 1)
            act.dma_start(ext_sb[0:HEADS, P - 1:P - 1 + N_REL], io["rel_bias_reversed"]
                          ).then_inc(rel_in, 16)
            for k in range(KD + WV_SLOTS):
                if k >= WV_SLOTS:
                    n = k - WV_SLOTS
                    act.wait_ge(wv_loaded[n % WV_SLOTS], 16 * (n // WV_SLOTS + 1))
                    nc.scalar.activation(wv_hi[:, n, :], wv_raw(n), ACT.Copy).then_inc(wvhi_ready, 1)
                if k < KD:
                    if k >= WV_SLOTS:
                        act.wait_ge(wvlo_ready, k - WV_SLOTS + 1)
                    act.dma_start(wv_raw(k), io["w_in"][bass.ts(k, P), 2 * DA:3 * DA]
                                  ).then_inc(wv_loaded[k % WV_SLOTS], 16)
            ext = scr["bias_ext"]
            act.wait_ge(ext_ready, 2)
            act.dma_start(ext, ext_sb[0:HEADS, :]).then_inc(bias_stored, 16)
            act.wait_ge(bias_stored, 16)
            act.dma_start(scr["bias_rows"].rearrange("p h m -> p (h m)"),
                          ext.rearrange("h m -> (h m)").partition_broadcast(P)).then_inc(bias_stored, 16)

            def body(at):
                if tile := at(TURN):
                    j, u = tile
                    t = 2 * j + u
                    whole(act, top, (transposed, t + 1 + CREDITS))
                    nc.scalar.activation(hT_hi[:, :, bass.ts(t, P)],
                                         tp[u][:, :].rearrange("p (k t) -> p k t", k=KD),
                                         ACT.Copy).then_inc(hhi_ready, 1)
                if tile := at(VALUE):
                    j, u = tile
                    t = 2 * j + u
                    act.wait_ge(v_ready, t + 1)
                    act.wait_ge(v_stored[u], 16 + 32 * j)
                    nc.scalar.activation(v_hi[:, u, :], vp[u][:, :], ACT.Copy).then_inc(vhi_ready, 1)

            ticks(act, TT, DEPTH1, body)

        @block.vector
        def _(dve):
            nc.vector.memset(ext_sb[0:HEADS, :], 0.0).then_inc(ext_ready, 1)
            dve.wait_ge(rel_in, 16)
            nc.vector.tensor_scalar(ext_sb[0:HEADS, 0:P - 1], ext_sb[0:HEADS, 0:P - 1],
                                    ext_sb[0:HEADS, P - 1:P], None, ALU.add).then_inc(ext_ready, 1)
            def split_weights(k):
                dve.wait_ge(wvhi_ready, k + 1)
                nc.vector.tensor_tensor(out=wv_lo[:, k, :], in0=wv_raw(k),
                                        in1=f32(wv_hi[:, k, :]), op=ALU.subtract).then_inc(wvlo_ready, 1)

            dve.wait_ge(rows_loaded, 32)

            def body(at):
                if tile := at(NORM):
                    j, u = tile
                    t = 2 * j + u
                    dve.wait_ge(rstd_ready, t + 1)
                    dve.wait_ge(transposed, t + 1)
                    dve.wait_ge(h_stored[u], 16 * (j + 1))
                    nc.vector.tensor_scalar(h_sb[:, u, :], x_sb[:, u, :], mean_var[:, u, 0:1],
                                            rstd[:, u, :], ALU.subtract, ALU.mult).then_inc(normed, 1)
                    dve.wait_ge(normed, t + 1 + CREDITS)
                    nc.vector.tensor_tensor(out=h_sb[:, u, :], in0=h_sb[:, u, :], in1=gain[:, :],
                                            op=ALU.mult).then_inc(gained, 1)
                if tile := at(STATS):
                    j, u = tile
                    t = 2 * j + u
                    dve.wait_ge(x_loaded[u], 16 * (j + 1))
                    nc.vector.bn_stats(stats[:, u, 0:6], x_sb[:, u, 0:D // 2])
                    nc.vector.bn_stats(stats[:, u, 6:12], x_sb[:, u, D // 2:D]).then_inc(stats_step, 1)
                    whole(dve, top, (stats_step, 2 * t + 1))
                    nc.vector.bn_aggr(mean_var[:, u, :], stats[:, u, :]).then_inc(stats_step, 1)
                    dve.wait_ge(stats_step, 2 * t + 2)
                    nc.vector.tensor_scalar(var_eps[:, u, :], mean_var[:, u, 1:2], EPS, None,
                                            ALU.add).then_inc(var_ready, 1)
                    if isinstance(t, int):
                        for k in range(3 * t, min(3 * t + 3, KD)):
                            split_weights(k)
                if tile := at(TURN):
                    j, u = tile
                    t = 2 * j + u
                    dve.wait_ge(hhi_ready, t + 1)
                    nc.vector.tensor_tensor(out=hT_lo[:, :, bass.ts(t, P)],
                                            in0=tp[u][:, :].rearrange("p (k t) -> p k t", k=KD),
                                            in1=f32(hT_hi[:, :, bass.ts(t, P)]),
                                            op=ALU.subtract).then_inc(hlo_ready, 1)
                if tile := at(VALUE):
                    j, u = tile
                    t = 2 * j + u
                    dve.wait_ge(vhi_ready, t + 1)
                    nc.vector.tensor_tensor(out=v_lo[:, u, :], in0=vp[u][:, :], in1=f32(v_hi[:, u, :]),
                                            op=ALU.subtract).then_inc(vlo_ready, 1)

            ticks(dve, TT, DEPTH1, body)

        @block.tensor
        def _(pe):
            pe.wait_ge(const1, 2)

            def body(at):
                if tile := at(TURN):
                    j, u = tile
                    t = 2 * j + u
                    pe.wait_ge(h_ready, t + 1)
                    pe.wait_ge(hlo_ready, t + 1)
                    for k in range(KD):
                        last = nc.tensor.transpose(tp[u][:, bass.ts(k, P)], h_sb[:, u, bass.ts(k, P)],
                                                   ident[:, :])
                    last.then_inc(transposed, 1)
                if tile := at(VALUE):
                    j, u = tile
                    t = 2 * j + u
                    if isinstance(t, int) and t == 0:
                        pe.wait_ge(wvlo_ready, KD)
                    pe.wait_ge(hlo_ready, t + 1 + CREDITS)
                    pe.wait_ge(vlo_ready, t + 1)
                    for k in range(KD):
                        last = three_passes(nc.tensor, vp[u][:, :], hT_hi[:, k, bass.ts(t, P)],
                                            hT_lo[:, k, bass.ts(t, P)],
                                            wv_hi[:, k, :], wv_lo[:, k, :], k == 0, k == KD - 1)
                    last.then_inc(v_ready, 1)

            for n in range(TT + DEPTH1 - 1):
                body(lambda k: divmod(n - k, 2) if 0 <= n - k < TT else None)
    m.stack.close()


CHUNK_COL = [4 * DA, 3 * DA, 0, DA]


def load_chunk(sp, io, w_raw, w_in, t, c):
    cols = io["w_in"][:, bass.ds(t * P + CHUNK_COL[c], P)]
    sp.dma_start(w_raw[:, c % 2, :, :], cols.rearrange("(k p) n -> p k n", p=P)).then_inc(w_in[c % 2], 16)


def phase2(nc, top, io, scr, hT_hi, hT_lo, w_raw, w_in):
    m = top.phase()
    w_hi = m.sb("w_hi2", [2, KD, P], F32R)
    w_lo = m.sb("w_lo2", [2, KD, P], F32R)
    xl = m.sb("xl", [CW - 1 + T])
    gl = m.sb("gelu_gate", [T])
    xc = m.sb("conv_out", [T])
    xc_hi = m.sb("xc_hi", [2, BLK], F32R)
    xc_lo = m.sb("xc_lo", [2, BLK], F32R)
    decay = m.sb("decay", [2, BLK])
    mult = m.sb("mult", [2, BLK])
    state = m.sb("state", [2, BLK])
    o_hi = m.sb("o_hi2", [2, BLK], F32R)
    o_lo = m.sb("o_lo2", [2, BLK], F32R)
    gw_raw = m.sb("gw_raw", [2, P])
    gw_hi = m.sb("gw_hi", [2, P], F32R)
    gw_lo = m.sb("gw_lo", [2, P], F32R)
    b_in = m.sb("b_in", [3 * NA + 2 * NA])
    vecs = m.sb("lru_vectors", [9, NA])
    TAP, CONV_B, B_A, B_X, LAMBDA, RATE = 0, 4, 5, 6, 7, 8
    sp_tmp = m.sb("softplus_tmp", [4, NA])
    mm = [m.ps(f"mm2_{i}", BLK) for i in range(2)]
    gate_r = [m.ps(f"gate_r{i}", BLK) for i in range(2)]
    gate_i = [m.ps(f"gate_i{i}", BLK) for i in range(2)]

    o_stored, evac = (top.sem(n, 2) for n in ("o_stored2", "evac2"))
    (consts_in, gw_in, gwhi, gw_split, whi, w_split, mm_ready, conv_step, conv_done, xchi,
     xclo, gates_ready, tanh_done, log_ready, exp_done, squared, m2_ready, sqrt_done, u_ready, h_ready,
     gl_free, y_ready, hi_ready, soft, soft_act, pad_ready) = (top.sem(n + "_2") for n in (
        "consts_in", "gw_in", "gwhi", "gw_split", "whi", "w_split", "mm_ready",
        "conv_step", "conv_done", "xchi", "xclo", "gates_ready", "tanh_done", "log_ready", "exp_done",
        "squared", "m2_ready", "sqrt_done", "u_ready", "h_ready", "gl_free", "y_ready", "hi_ready",
        "soft", "soft_act", "pad_ready"))
    GATE, XIN, QUERY, KEY = range(4)
    ITEMS = 12
    MM0 = 2 * NB
    A, B, C, DD = "gates to log decay", "decay and input", "scan", "split"
    BESIDE = {(XIN, 3): [(A, 0)], (QUERY, 0): [(B, 0), (A, 1)], (QUERY, 1): [(C, 0), (B, 1)],
              (QUERY, 2): [(DD, 0), (C, 1)], (QUERY, 3): [(DD, 1), (A, 2)], (KEY, 0): [(B, 2), (A, 3)],
              (KEY, 1): [(C, 2), (B, 3)], (KEY, 2): [(DD, 2), (C, 3)], (KEY, 3): [(DD, 3)]}
    GATES = {(XIN, 2): 0, (XIN, 3): 1, (QUERY, 2): 2, (QUERY, 3): 3}
    XC_SPLIT = {(XIN, 1): 0, (XIN, 2): 1, (QUERY, 0): 2, (QUERY, 1): 3}
    ORDER = [(QUERY, 0), (QUERY, 1), (QUERY, 2), (DD, 0), (QUERY, 3), (DD, 1), (KEY, 0), (KEY, 1),
             (KEY, 2), (DD, 2), (KEY, 3), (DD, 3)]

    def item_of(chunk, b):
        return ORDER.index((chunk, b))

    with nc.Block() as block:
        @block.sync
        def _(sp):
            for s, n in ((w_split, CREDITS), (mm_ready, MM0), (conv_done, 1), (gl_free, NB),
                         (u_ready, CREDITS), (gw_split, 1), (gates_ready, CREDITS),
                         (h_ready, CREDITS)):
                sp.sem_inc(s, n)
            for u in range(2):
                sp.sem_inc(o_stored[u], 16)
                sp.sem_inc(evac[u], 1)

            def load(n, t, c):
                whole(sp, top, (w_split, n + 1))
                load_chunk(sp, io, w_raw, w_in, t, c)

            def body(t):
                last = isinstance(t, int)

                def store(name, chunk, b, k0):
                    i = item_of(chunk, b)
                    if chunk == DD:
                        whole(sp, top, (gl_free, NB * t + b + 1 + NB))
                    else:
                        whole(sp, top, (evac[b % 2], 1 + 8 * t + 2 * chunk + b // 2 + 1))
                    for part, src in ((0, o_hi), (1, o_lo)):
                        sp.dma_start(scr[name][part, bass.ds(t + k0, 1), :, bass.ts(b, BLK)]
                                     .rearrange("k p t -> p (k t)"),
                                     f32(src[:, i % 2, :])).then_inc(o_stored[i % 2], 16)

                whole(sp, top, (gw_split, t + 1))
                sp.dma_start(gw_raw[:, :, :], io["gate_w"][bass.ds(t, 1), :, :, :]
                             .rearrange("t p g n -> p (t g) n")).then_inc(gw_in, 16)
                for c in range(4):
                    if not (last and c >= 2):
                        load(4 * t + c + 2, t + (c + 2) // 4, (c + 2) % 4)
                    for b in range(NB):
                        if c == QUERY:
                            store("q", QUERY, b, 0)
                        if c == KEY:
                            store("k", KEY, b, 0)
                        for stage, sb in BESIDE.get((c, b), ()):
                            if stage == DD:
                                store("yT", DD, sb, NA)

            rounds(sp, NA, body)
        @block.gpsimd
        def _(pool):
            nc.gpsimd.memset(xl[:, 0:CW - 1], 0.0).then_inc(pad_ready, 1)

        @block.scalar
        def _(act):
            act.dma_start(b_in[:, :], io["b_in"]).then_inc(consts_in, 16)
            act.dma_start(vecs[:, 0:8, :], io["lru_vectors"]).then_inc(consts_in, 16)

            def hi(t, c):
                act.wait_ge(w_in[c % 2], 32 * t + 16 * (c // 2 + 1))
                act.wait_ge(mm_ready, 16 * t + 4 * c - 4 + MM0)
                nc.scalar.activation(w_hi[:, c % 2, :, :].rearrange("p k n -> p (k n)"),
                                     w_raw[:, c % 2, :, :].rearrange("p k n -> p (k n)"),
                                     ACT.Copy).then_inc(whi, 1)

            hi(0, GATE)
            act.wait_ge(soft, 1)
            nc.scalar.activation(sp_tmp[:, 1, :], sp_tmp[:, 0, :], ACT.Exp, scale=-1.0).then_inc(soft_act, 1)
            act.wait_ge(consts_in, 32)

            def body(t):
                last = isinstance(t, int)

                def split_hi(chunk, b, src, bias, source_ready):
                    i = item_of(chunk, b)
                    whole(act, top, source_ready,
                          (o_stored[i % 2], 16 + 32 * (ITEMS // 2 * t + i // 2)))
                    nc.scalar.activation(o_hi[:, i % 2, :], src, ACT.Identity, bias=bias
                                         ).then_inc(hi_ready, 1)

                for c in range(4):
                    for b in range(NB):
                        product = (mm_ready, 16 * t + 4 * c + b + 1 + MM0)
                        if c == GATE:
                            whole(act, top, product, (gl_free, NB * t + b + 1))
                            nc.scalar.activation(gl[:, bass.ts(b, BLK)], mm[b % 2][:, :],
                                                 ACT.Gelu_apprx_tanh,
                                                 bias=b_in[:, bass.ds(t + 4 * NA, 1)]
                                                 ).then_inc(evac[b % 2], 1)
                        if c == XIN:
                            whole(act, top, product, (conv_done, NB * t + 1))
                            nc.scalar.activation(xl[:, bass.ds(CW - 1 + b * BLK, BLK)], mm[b % 2][:, :],
                                                 ACT.Identity, bias=b_in[:, bass.ds(t + 3 * NA, 1)]
                                                 ).then_inc(evac[b % 2], 1)
                        if c == QUERY:
                            split_hi(QUERY, b, mm[b % 2][:, :], b_in[:, bass.ds(t, 1)], product)
                        if c == KEY:
                            split_hi(KEY, b, mm[b % 2][:, :], b_in[:, bass.ds(t + NA, 1)], product)
                        if b == 0 and not (last and c == KEY):
                            hi(t + (c + 1) // 4, (c + 1) % 4)
                        if c == XIN and b == 0:
                            act.wait_ge(gw_in, 16 * t + 16)
                            act.wait_ge(gates_ready, NB * t + CREDITS)
                            nc.scalar.activation(gw_hi[:, :, :], gw_raw[:, :, :], ACT.Copy
                                                 ).then_inc(gwhi, 1)
                        if (c, b) in XC_SPLIT:
                            sb = XC_SPLIT[c, b]
                            act.wait_ge(conv_done, NB * t + sb + 2)
                            act.wait_ge(gates_ready, NB * t + sb + 1)
                            nc.scalar.activation(xc_hi[:, sb % 2, :], xc[:, bass.ts(sb, BLK)], ACT.Copy
                                                 ).then_inc(xchi, 1)
                        for stage, sb in BESIDE.get((c, b), ()):
                            s = sb % 2
                            if stage == A:
                                whole(act, top, (gates_ready, NB * t + sb + 1 + CREDITS))
                                nc.scalar.activation(gate_r[s][:, :], gate_r[s][:, :], ACT.Tanh, scale=0.5,
                                                     bias=vecs[:, B_A, bass.ds(t, 1)]).then_inc(tanh_done, 1)
                                nc.scalar.activation(gate_i[s][:, :], gate_i[s][:, :], ACT.Tanh, scale=0.5,
                                                     bias=vecs[:, B_X, bass.ds(t, 1)]).then_inc(tanh_done, 1)
                            if stage == B:
                                act.wait_ge(log_ready, NB * t + sb + 1)
                                act.wait_ge(h_ready, NB * t + sb + 1)
                                nc.scalar.activation(decay[:, s, :], gate_r[s][:, :], ACT.Exp
                                                     ).then_inc(exp_done, 1)
                                act.wait_ge(exp_done, 2 * (NB * t + sb) + 1)
                                nc.scalar.activation(gate_r[s][:, :], gate_r[s][:, :], ACT.Tanh, scale=-1.0
                                                     ).then_inc(exp_done, 1)
                            if stage == C:
                                act.wait_ge(m2_ready, NB * t + sb + 1)
                                nc.scalar.activation(mult[:, s, :], mult[:, s, :], ACT.Sqrt, scale=0.25
                                                     ).then_inc(sqrt_done, 1)
                            if stage == DD:
                                split_hi(DD, sb, gl[:, bass.ts(sb, BLK)], 0.0,
                                         (y_ready, NB * t + sb + 1))

            rounds(act, NA, body)

        @block.vector
        def _(dve):
            def lo(t, c):
                dve.wait_ge(whi, 4 * t + c + 1)
                nc.vector.tensor_tensor(out=w_lo[:, c % 2, :, :].rearrange("p k n -> p (k n)"),
                                        in0=w_raw[:, c % 2, :, :].rearrange("p k n -> p (k n)"),
                                        in1=f32(w_hi[:, c % 2, :, :]).rearrange("p k n -> p (k n)"),
                                        op=ALU.subtract).then_inc(w_split, 1)

            lo(0, GATE)

            dve.wait_ge(consts_in, 32)
            lam, e, z, z2, acc = (vecs[:, LAMBDA, :], sp_tmp[:, 1, :], sp_tmp[:, 2, :], sp_tmp[:, 3, :],
                                  vecs[:, RATE, :])
            nc.vector.scalar_tensor_tensor(sp_tmp[:, 0, :], lam, -1.0, lam, ALU.mult, ALU.max
                                           ).then_inc(soft, 1)
            dve.wait_ge(soft_act, 1)
            n = 1

            def chain(instruction):
                nonlocal n
                instruction.then_inc(soft, 1)
                n += 1
                dve.wait_ge(soft, n)

            chain(nc.vector.tensor_scalar(z2, e, 2.0, None, ALU.add))
            chain(nc.vector.reciprocal(z, z2))
            chain(nc.vector.tensor_tensor(out=z, in0=z, in1=e, op=ALU.mult))
            chain(nc.vector.tensor_tensor(out=z2, in0=z, in1=z, op=ALU.mult))
            chain(nc.vector.tensor_scalar(acc, z2, 1.0 / 17, 1.0 / 15, ALU.mult, ALU.add))
            for d in (13, 11, 9, 7, 5, 3, 1):
                chain(nc.vector.tensor_tensor(out=acc, in0=acc, in1=z2, op=ALU.mult))
                chain(nc.vector.tensor_scalar(acc, acc, 1.0 / d, None, ALU.add))
            chain(nc.vector.tensor_tensor(out=acc, in0=acc, in1=z, op=ALU.mult))
            chain(nc.vector.tensor_scalar(z, lam, -0.5, 0.0, ALU.mult, ALU.max))
            chain(nc.vector.tensor_tensor(out=acc, in0=acc, in1=z, op=ALU.add))
            chain(nc.vector.tensor_scalar(acc, acc, -LRU_C, None, ALU.mult))
            chain(nc.vector.tensor_scalar(vecs[:, B_A:B_X + 1, :], vecs[:, B_A:B_X + 1, :], 0.5, None,
                                          ALU.mult))
            dve.wait_ge(pad_ready, 1)

            def body(t):
                last = isinstance(t, int)
                vec = lambda row: vecs[:, row, bass.ds(t, 1)]

                def split_lo(chunk, b, src, bias):
                    i = item_of(chunk, b)
                    dve.wait_ge(hi_ready, ITEMS * t + i + 1)
                    return nc.vector.scalar_tensor_tensor(o_lo[:, i % 2, :], src, bias,
                                                          f32(o_hi[:, i % 2, :]), ALU.add, ALU.subtract)

                for c in range(4):
                    for b in range(NB):
                        if c == QUERY:
                            split_lo(QUERY, b, mm[b % 2][:, :], b_in[:, bass.ds(t, 1)]
                                     ).then_inc(evac[b % 2], 1)
                        if c == KEY:
                            split_lo(KEY, b, mm[b % 2][:, :], b_in[:, bass.ds(t + NA, 1)]
                                     ).then_inc(evac[b % 2], 1)
                        if b == 0 and not (last and c == KEY):
                            lo(t + (c + 1) // 4, (c + 1) % 4)
                        if c == XIN:
                            if b == 0:
                                dve.wait_ge(gwhi, t + 1)
                                nc.vector.tensor_tensor(out=gw_lo[:, :, :], in0=gw_raw[:, :, :],
                                                        in1=f32(gw_hi[:, :, :]), op=ALU.subtract
                                                        ).then_inc(gw_split, 1)
                            dve.wait_ge(evac[b % 2], 1 + 8 * t + 2 + b // 2 + 1)
                            out = xc[:, bass.ts(b, BLK)]
                            nc.vector.tensor_scalar(out, xl[:, bass.ds(b * BLK, BLK)], vec(TAP),
                                                    vec(CONV_B), ALU.mult, ALU.add).then_inc(conv_step, 1)
                            for k in range(1, CW):
                                dve.wait_ge(conv_step, (CW - 1) * (NB * t + b) + k)
                                nc.vector.scalar_tensor_tensor(
                                    out, xl[:, bass.ds(b * BLK + k, BLK)], vec(TAP + k), out,
                                    ALU.mult, ALU.add).then_inc(conv_step if k < CW - 1 else conv_done, 1)
                        if (c, b) in XC_SPLIT:
                            sb = XC_SPLIT[c, b]
                            dve.wait_ge(xchi, NB * t + sb + 1)
                            nc.vector.tensor_tensor(out=xc_lo[:, sb % 2, :], in0=xc[:, bass.ts(sb, BLK)],
                                                    in1=f32(xc_hi[:, sb % 2, :]), op=ALU.subtract
                                                    ).then_inc(xclo, 1)
                        for stage, sb in BESIDE.get((c, b), ()):
                            s = sb % 2
                            i = NB * t + sb
                            if stage == A:
                                dve.wait_ge(tanh_done, 2 * i + 2)
                                nc.vector.tensor_scalar(gate_r[s][:, :], gate_r[s][:, :], 1.0, vec(RATE),
                                                        ALU.add, ALU.mult).then_inc(log_ready, 1)
                                nc.vector.scalar_tensor_tensor(gate_i[s][:, :], gate_i[s][:, :], 1.0,
                                                               xc[:, bass.ts(sb, BLK)], ALU.add, ALU.mult
                                                               )
                            if stage == B:
                                dve.wait_ge(exp_done, 2 * i + 2)
                                nc.vector.tensor_tensor(out=mult[:, s, :], in0=decay[:, s, :],
                                                        in1=decay[:, s, :], op=ALU.mult).then_inc(squared, 1)
                                dve.wait_ge(squared, i + 1)
                                nc.vector.scalar_tensor_tensor(mult[:, s, :], mult[:, s, :], 1.0,
                                                               gate_r[s][:, :], ALU.add, ALU.mult
                                                               ).then_inc(m2_ready, 1)
                            if stage == C:
                                dve.wait_ge(sqrt_done, i + 1)
                                nc.vector.tensor_tensor(out=mult[:, s, :], in0=gate_i[s][:, :],
                                                        in1=mult[:, s, :], op=ALU.mult).then_inc(u_ready, 1)
                                dve.wait_ge(u_ready, i + 1 + CREDITS)
                                before = 0.0 if sb == 0 else state[:, 1 - s, BLK - 1:BLK]
                                nc.vector.tensor_tensor_scan(state[:, s, :], decay[:, s, :], mult[:, s, :],
                                                             before, ALU.mult, ALU.add).then_inc(h_ready, 1)
                                dve.wait_ge(h_ready, i + 1 + CREDITS)
                                nc.vector.tensor_tensor(out=gl[:, bass.ts(sb, BLK)], in0=state[:, s, :],
                                                        in1=gl[:, bass.ts(sb, BLK)], op=ALU.mult
                                                        ).then_inc(y_ready, 1)
                            if stage == DD:
                                split_lo(DD, sb, gl[:, bass.ts(sb, BLK)], 0.0).then_inc(gl_free, 1)

            rounds(dve, NA, body)

        @block.tensor
        def _(pe):
            def body(t):
                for c in range(4):
                    pe.wait_ge(w_split, 4 * t + c + 1 + CREDITS)
                    for b in range(NB):
                        pe.wait_ge(evac[b % 2], 8 * t + 2 * c + b // 2 + 1)
                        for k in range(KD):
                            last = three_passes(nc.tensor, mm[b % 2][:, :], w_hi[:, c % 2, k, :],
                                                w_lo[:, c % 2, k, :], hT_hi[:, k, bass.ts(b, BLK)],
                                                hT_lo[:, k, bass.ts(b, BLK)], k == 0, k == KD - 1)
                        last.then_inc(mm_ready, 1)
                        if (c, b) in GATES:
                            gb = GATES[c, b]
                            s = gb % 2
                            pe.wait_ge(xclo, NB * t + gb + 1)
                            pe.wait_ge(gw_split, t + 2)
                            pe.wait_ge(u_ready, NB * t + gb + 1)
                            three_passes(nc.tensor, gate_r[s][:, :], gw_hi[:, 0, :], gw_lo[:, 0, :],
                                         xc_hi[:, s, :], xc_lo[:, s, :], True, True)
                            three_passes(nc.tensor, gate_i[s][:, :], gw_hi[:, 1, :], gw_lo[:, 1, :],
                                         xc_hi[:, s, :], xc_lo[:, s, :], True, True
                                         ).then_inc(gates_ready, 1)

            rounds(pe, NA, body)
    m.stack.close()
    return [(o_stored[u], 16 + 32 * ITEMS * n // 2) for n in (1, NA) for u in range(2)]


def sweep(eng, rounds_, steps, depth, body):
    def fixed(n):
        return lambda k: divmod(n - k, steps) if 0 <= n - k < rounds_ * steps else None

    for n in range(depth):
        body(fixed(n))
    with eng.Fori(0, rounds_ - 1) as g:
        for n in range(depth, depth + steps):
            body(lambda k, n=n: (g + (n - k) // steps, (n - k) % steps))
    for n in range(depth + steps * (rounds_ - 1), depth + steps * rounds_):
        body(fixed(n))


def phase3(nc, top, io, scr, stored, load_next):
    m = top.phase()
    q_hi, q_lo, k_hi, k_lo = (m.sb(n, [T], F32R) for n in ("q_hi", "q_lo", "k_hi", "k_lo"))
    v_hi = m.sb("v_hi3", [TT, P], F32R)
    v_lo = m.sb("v_lo3", [TT, P], F32R)
    near = m.sb("near", [HEADS, NEAR])
    far = m.sb("bias_far", [HEADS])
    b_in = m.sb("b_in3", [3 * NA + 2 * NA])
    probs = m.sb("probs", [4, 2 * BLK])
    pT_hi = m.sb("pT_hi", [2, 2 * TPB, BLK], F32R)
    pT_lo = m.sb("pT_lo", [2, 2 * TPB, BLK], F32R)
    y_hi = m.sb("y_hi3", [2, BLK], F32R)
    y_lo = m.sb("y_lo3", [2, BLK], F32R)
    ident = m.sb("ident3", [P])
    mask_f = m.sb("mask_f32", [P + CHUNK])
    mask = m.sb("mask", [P + CHUNK], F32R)
    top_score, neg_max, total, inv_total = (m.sb(n, [4, 1]) for n in (
        "top_score", "neg_max", "total", "inv_total"))
    score = [m.ps(f"score{i}", 2 * BLK) for i in range(2)]
    turned_p = [m.ps(f"probs_transposed{i}", BLK) for i in range(2)]
    av = [m.ps(f"attended{i}", BLK) for i in range(2)]

    qkv_in = top.sem("qkv_in", NB)
    y_stored = top.sem("y_stored3", 2)
    turned, pT_hi_done, pT_lo_done = (top.sem(n + "_3", 2) for n in (
        "turned", "pT_hi_done", "pT_lo_done"))
    (bias_in, consts_in, const, table_step, qk_done, top_step, neg_max_ready,
     exp_done, inv_ready, normed, av_done, y_hi_done, y_lo_done) = (top.sem(n + "_3") for n in (
        "bias_in", "consts_in", "const", "table_step", "qk_done", "top_step",
        "neg_max_ready", "exp_done", "inv_ready", "normed", "av_done", "y_hi_done", "y_lo_done"))
    STEPS = NB * 2 * TPB
    GROUPS = NB * 2
    SLOTS = 4
    SCORE, EXP, INVERT, NORM, TURN, SPLIT, ATTEND, OUT, DEPTH3 = 0, 1, 2, 3, 3, 4, 8, 12, 13

    def parts(s):
        return s // (2 * TPB), s // TPB % 2, s % TPB

    def columns(b, i):
        first = (i if b > 0 else TPB) * P
        return first, (i + TPB + 1) * P

    def halves(s):
        b, _, i = parts(s)
        lo, hi = columns(b, i)
        cut = lo + ((hi - lo) // P + 1) // 2 * P
        return [(0, lo, cut), (1, cut, hi)] if cut < hi else [(0, lo, cut)]

    def halves_before(g, s, half):
        have = [len(halves(r)) > half for r in range(STEPS)]
        return sum(have) * (g + s // STEPS) + sum(have[:s % STEPS])

    with nc.Block() as block:
        @block.sync
        def _(sp):
            for s, n in ((exp_done, CREDITS), (turned[0], SLOTS), (turned[1], SLOTS),
                         (pT_lo_done[0], 1), (pT_lo_done[1], 1), (av_done, CREDITS), (y_lo_done, CREDITS)):
                sp.sem_inc(s, n)
            for u in range(2):
                sp.sem_inc(y_stored[u], 16)

            def load(g, b):
                for name, dsts in (("q", (q_hi, q_lo)), ("k", (k_hi, k_lo))):
                    for part, dst in enumerate(dsts):
                        sp.dma_start(f32(dst[:, bass.ts(b, BLK)]),
                                     scr[name][part, bass.ds(g, 1), :, bass.ts(b, BLK)]
                                     .rearrange("k p t -> p (k t)")).then_inc(qkv_in[b], 16)
                for part, dst in enumerate((v_hi, v_lo)):
                    sp.dma_start(f32(dst[:, bass.ts(b, TPB), :]),
                                 scr["v"][part, bass.ts(b, BLK), bass.ds(g * P, P)]
                                 .rearrange("(j p) n -> p j n", p=P)).then_inc(qkv_in[b], 16)

            for sem, count in stored[:2]:
                sp.wait_ge(sem, count)
            for b in range(NB):
                load(0, b)
            for sem, count in stored[2:]:
                sp.wait_ge(sem, count)

            def body(g):
                last = isinstance(g, int)
                if last:
                    load_next(sp)
                for b in range(NB):
                    whole(sp, top, (y_lo_done, GROUPS * g + 2 * b + 2 + CREDITS))
                    for part, src in ((0, y_hi), (1, y_lo)):
                        sp.dma_start(scr["yT"][part, bass.ds(g, 1), :, bass.ts(b, BLK)]
                                     .rearrange("k p t -> p (k t)"),
                                     f32(src[:, b % 2, :])).then_inc(y_stored[b % 2], 16)
                    if not last:
                        if b > 0:
                            load(g + 1, b - 1)
                        if b == NB - 1:
                            load(g + 1, b)

            rounds(sp, NA, body)
            for u in range(2):
                sp.wait_ge(y_stored[u], 16 + 32 * NA * NB // 2)

        @block.gpsimd
        def _(pool):
            identity(nc, pool, ident, const)
            nc.gpsimd.memset(mask_f[0:1, 0:CHUNK], 0.0).then_inc(const, 1)
            nc.gpsimd.memset(mask_f[0:1, CHUNK:P], NEG).then_inc(const, 1)
            nc.gpsimd.memset(mask_f[0:1, P:P + CHUNK], 1.0).then_inc(const, 1)

        @block.scalar
        def _(act):
            toeplitz = bass.AP(tensor=scr["bias_rows"].tensor, offset=P - 1,
                               ap=[[HEADS * BIAS_EXT - 1, P], [BIAS_EXT, HEADS], [1, NEAR]])
            act.dma_start(near[:, :, :], toeplitz).then_inc(bias_in, 16)
            act.dma_start(far[:, :], io["bias_far"].partition_broadcast(P)).then_inc(bias_in, 16)
            act.dma_start(b_in[:, :], io["b_in"]).then_inc(consts_in, 16)
            act.wait_ge(const, 5)
            nc.scalar.activation(mask[0:1, :], mask_f[0:1, :], ACT.Copy).then_inc(const, 1)
            act.wait_ge(consts_in, 16)

            def body(at):
                if step := at(NORM):
                    g, s = step
                    b, h, i = parts(s)
                    lo, hi = columns(b, i)
                    p = s % SLOTS
                    act.wait_ge(inv_ready, STEPS * g + s + 1)
                    nc.scalar.activation(probs[:, p, lo:hi], probs[:, p, lo:hi], ACT.Copy,
                                         scale=inv_total[:, p, :]).then_inc(normed, 1)
                if step := at(SPLIT):
                    g, s = step
                    u = s // TPB % 2
                    for half, lo, hi in halves(s):
                        act.wait_ge(turned[half], halves_before(g, s, half) + 1 + SLOTS)
                        if half == 0:
                            act.wait_ge(av_done, GROUPS * g + s // TPB + 1)
                        nc.scalar.activation(
                            pT_hi[:, u, lo // P:hi // P, bass.ts(s % TPB, P)],
                            turned_p[half][:, 0:hi - lo].rearrange("p (j q) -> p j q", q=P), ACT.Copy
                        ).then_inc(pT_hi_done[half], 1)
                if step := at(EXP):
                    g, s = step
                    b, h, i = parts(s)
                    n = STEPS * g + s
                    lo, hi = columns(b, i)
                    act.wait_ge(neg_max_ready, n + 1)
                    for half in range(2):
                        act.wait_ge(turned[half], halves_before(g - 1, s + 1 + STEPS - SLOTS, half)
                                    + SLOTS)
                    nc.scalar.activation(probs[:, s % SLOTS, lo:hi], score[s % 2][:, lo:hi], ACT.Exp,
                                         scale=SCALE, bias=neg_max[:, s % SLOTS, :],
                                         accum_out=total[:, s % SLOTS, :]).then_inc(exp_done, 1)
                if (step := at(OUT)) and step[1] % TPB == 0:
                    g, s = step
                    b, h, _ = parts(s)
                    rows = slice(HD * h, HD * h + HD)
                    whole(act, top, (av_done, GROUPS * g + s // TPB + 1 + CREDITS),
                          (y_stored[b % 2], 16 + 32 * (NB // 2 * g + b // 2)))
                    nc.scalar.activation(y_hi[rows, b % 2, :], av[h][rows, :], ACT.Identity,
                                         bias=b_in[rows, bass.ds(g + 2 * NA, 1)]
                                         ).then_inc(y_hi_done, 1)

            sweep(act, NA, STEPS, DEPTH3, body)

        @block.vector
        def _(dve):
            dve.wait_ge(bias_in, 32)
            for h in range(HEADS):
                nc.vector.tensor_scalar(near[:, h, :], near[:, h, :], far[:, h:h + 1], 1.0 / SCALE,
                                        ALU.subtract, ALU.mult).then_inc(table_step, 1)
            dve.wait_ge(table_step, HEADS)
            nc.vector.memset(near[0:CHUNK, :, NEAR - CHUNK:NEAR], NEG).then_inc(table_step, 1)
            dve.wait_ge(table_step, HEADS + 1)
            dve.wait_ge(consts_in, 16)

            def body(at):
                if step := at(INVERT):
                    g, s = step
                    n = STEPS * g + s
                    dve.wait_ge(exp_done, n + 1 + CREDITS)
                    nc.vector.reciprocal(inv_total[:, s % SLOTS, :], total[:, s % SLOTS, :]
                                         ).then_inc(inv_ready, 1)
                if step := at(SPLIT):
                    g, s = step
                    u = s // TPB % 2
                    for half, lo, hi in halves(s):
                        tiles, queries = slice(lo // P, hi // P), bass.ts(s % TPB, P)
                        dve.wait_ge(pT_hi_done[half], halves_before(g, s, half) + 1)
                        nc.vector.tensor_tensor(
                            out=pT_lo[:, u, tiles, queries],
                            in0=turned_p[half][:, 0:hi - lo].rearrange("p (j q) -> p j q", q=P),
                            in1=f32(pT_hi[:, u, tiles, queries]), op=ALU.subtract
                        ).then_inc(pT_lo_done[half], 1)
                if step := at(SCORE):
                    g, s = step
                    b, h, i = parts(s)
                    n = STEPS * g + s
                    lo, hi = columns(b, i)
                    p = s % SLOTS
                    sc = score[s % 2]
                    cut = max(lo, hi - NEAR)
                    dve.wait_ge(qk_done, n + 1)
                    nc.vector.tensor_tensor(
                        out=sc[:, cut:hi], in0=sc[:, cut:hi],
                        in1=near[:, bass.ds(2 * g + h, 1), NEAR - (hi - cut):NEAR]
                        .rearrange("p h c -> p (h c)"), op=ALU.add).then_inc(top_step, 1)
                    dve.wait_ge(top_step, 2 * n + 1)
                    nc.vector.tensor_reduce(top_score[:, p, :], sc[:, lo:hi], AX.X, ALU.max
                                            ).then_inc(top_step, 1)
                    dve.wait_ge(top_step, 2 * n + 2)
                    nc.vector.tensor_scalar(neg_max[:, p, :], top_score[:, p, :], -SCALE, None,
                                            ALU.mult).then_inc(neg_max_ready, 1)
                if (step := at(OUT)) and step[1] % TPB == 0:
                    g, s = step
                    b, h, _ = parts(s)
                    rows = slice(HD * h, HD * h + HD)
                    dve.wait_ge(y_hi_done, GROUPS * g + s // TPB + 1)
                    nc.vector.scalar_tensor_tensor(y_lo[rows, b % 2, :], av[h][rows, :],
                                                   b_in[rows, bass.ds(g + 2 * NA, 1)],
                                                   f32(y_hi[rows, b % 2, :]), ALU.add, ALU.subtract
                                                   ).then_inc(y_lo_done, 1)

            sweep(dve, NA, STEPS, DEPTH3, body)

        @block.tensor
        def _(pe):
            pe.wait_ge(const, 6)

            def body(at):
                if step := at(SCORE):
                    g, s = step
                    b, h, i = parts(s)
                    n = STEPS * g + s
                    sc = score[s % 2]
                    rows = slice(HD * h, HD * h + HD)
                    queries = slice(b * BLK + i * P, b * BLK + (i + 1) * P)
                    if s % (2 * TPB) == 0:
                        pe.wait_ge(qkv_in[b], 96 * g + 96)
                    pe.wait_ge(exp_done, n + 1)
                    if b > 0:
                        lo = i * P
                        keys = slice((b - 1) * BLK + i * P, b * BLK)
                        out = sc[:, lo:BLK]
                        nc.tensor.matmul(out, q_hi[rows, queries], k_hi[rows, keys], start=True, stop=False)
                        nc.tensor.matmul(sc[:, lo:lo + CHUNK], mask[0:1, 0:P], mask[0:1, P:P + CHUNK],
                                         start=False, stop=False)
                        nc.tensor.matmul(out, q_hi[rows, queries], k_lo[rows, keys], start=False, stop=False)
                        nc.tensor.matmul(out, q_lo[rows, queries], k_hi[rows, keys], start=False, stop=True)
                    keys = slice(b * BLK, b * BLK + (i + 1) * P)
                    three_passes(nc.tensor, sc[:, BLK:BLK + (i + 1) * P], q_hi[rows, queries],
                                 q_lo[rows, queries], k_hi[rows, keys], k_lo[rows, keys], True, True
                                 ).then_inc(qk_done, 1)
                if step := at(ATTEND):
                    g, s = step
                    b, h, part = parts(s)
                    group = GROUPS * g + s // TPB
                    order = [TPB + j for j in range(TPB)] + [j for j in range(TPB) if b > 0]
                    per = len(order) // TPB
                    if part == 0:
                        for half in range(2):
                            pe.wait_ge(pT_lo_done[half], halves_before(g, s + TPB, half) + 1)
                        pe.wait_ge(y_lo_done, group + 1)
                    for n in range(part * per, (part + 1) * per):
                        j = order[n]
                        tile = b * TPB + j - TPB
                        cols = slice((j - TPB) * P, BLK) if j >= TPB else slice(0, (j + 1) * P)
                        last = three_passes(nc.tensor, av[h][:, cols], v_hi[:, tile, :], v_lo[:, tile, :],
                                            pT_hi[:, h, j, cols], pT_lo[:, h, j, cols],
                                            n == 0, n == len(order) - 1)
                    if part == TPB - 1:
                        last.then_inc(av_done, 1)
                if step := at(TURN):
                    g, s = step
                    pe.wait_ge(normed, STEPS * g + s + 1)
                    for half, lo, hi in halves(s):
                        pe.wait_ge(pT_lo_done[half], halves_before(g, s, half) + 1)
                        for c in range(lo, hi, P):
                            last = nc.tensor.transpose(turned_p[half][:, c - lo:c - lo + P],
                                                       probs[:, s % SLOTS, c:c + P], ident[:, :])
                        last.then_inc(turned[half], 1)

            sweep(pe, NA, STEPS, DEPTH3, body)
    m.stack.close()


def phase4(nc, top, io, scr, w_raw, w_in, load_next):
    m = top.phase()
    w_hi = m.sb("wo_hi", [KD, D], F32R)
    w_lo = m.sb("wo_lo", [KD, D], F32R)
    y_hi = m.sb("y_hi", [2, KD, P], F32R)
    y_lo = m.sb("y_lo", [2, KD, P], F32R)
    h0 = m.sb("h0_tile", [2, D])
    res = m.sb("residual4", [2, D])
    h1 = m.sb("h1_tile", [2, D])
    h1T_hi = m.sb("h1T_hi", [2, KD, P], F32R)
    h1T_lo = m.sb("h1T_lo", [2, KD, P], F32R)
    bias = m.sb("b_out_row", [D])
    gain = m.sb("ln1_gain", [D])
    shift = m.sb("ln1_shift", [D])
    ident = m.sb("ident4", [P])
    stats = m.sb("stats4", [2, 12])
    mean_var = m.sb("mean_var4", [2, 2])
    var_eps = m.sb("var_eps4", [2, 1])
    minus_half = m.sb("minus_half4", [1])
    rstd = m.sb("rstd4", [2, 1])
    mix = [m.ps(f"mix{i}", D) for i in range(2)]
    tp = [m.ps(f"h1_transposed{i}", D) for i in range(2)]

    y_in, h0_in, h1_stored, h1T_stored = (top.sem(n, 2) for n in (
        "y_in4", "h0_in4", "h1_stored4", "h1T_stored4"))
    (rows_in, const, whi, wlo, mixed, summed, carried, stats_step, var_ready, rstd_ready,
     normed, gained, h1_ready, transposed, hhi_ready, hlo_ready) = (top.sem(n + "_4") for n in (
        "rows_in", "const", "whi", "wlo", "mixed", "summed", "carried", "stats_step",
        "var_ready", "rstd_ready", "normed", "gained", "h1_ready", "transposed", "hhi_ready",
        "hlo_ready"))
    DEPTH4 = 6
    LOAD, MIX, STATS, NORM, TURN, STORE = range(DEPTH4)

    with nc.Block() as block:
        @block.sync
        def _(sp):
            for s in (summed, normed, transposed, hlo_ready):
                sp.sem_inc(s, CREDITS)
            for u in range(2):
                sp.sem_inc(h1_stored[u], 16)
                sp.sem_inc(h1T_stored[u], 16)

            def body(at):
                if tile := at(STORE):
                    j, u = tile
                    t = 2 * j + u
                    whole(sp, top, (hlo_ready, t + 1 + CREDITS))
                    for part, src in ((0, h1T_hi), (1, h1T_lo)):
                        sp.dma_start(scr["h1T"][part, :, :, bass.ts(t, P)].rearrange("k p t -> p k t"),
                                     f32(src[:, u, :, :])).then_inc(h1T_stored[u], 16)
                if tile := at(LOAD):
                    j, u = tile
                    t = 2 * j + u
                    whole(sp, top, (summed, t + 1))
                    for part, dst in ((0, y_hi), (1, y_lo)):
                        sp.dma_start(f32(dst[:, u, :, :]),
                                     scr["yT"][part, :, :, bass.ts(t, P)].rearrange("k p t -> p k t")
                                     ).then_inc(y_in[u], 16)
                    sp.dma_start(h0[:, u, :], scr["h0"][bass.ts(t, P), :]).then_inc(h0_in[u], 16)
                if tile := at(NORM):
                    j, u = tile
                    t = 2 * j + u
                    whole(sp, top, (h1_ready, t + 1))
                    sp.dma_start(scr["h1"][bass.ts(t, P), :], h1[:, u, :]).then_inc(h1_stored[u], 16)
                    if isinstance(t, int) and t == TT - 3:
                        for u in range(2):
                            sp.wait_ge(h1T_stored[u], 16 + 32 * TPB // 2)
                        load_next(sp)

            ticks(sp, TT, DEPTH4, body)
        @block.gpsimd
        def _(pool):
            identity(nc, pool, ident, const)
            nc.gpsimd.memset(minus_half[:, :], -0.5).then_inc(const, 1)
            pool.wait_ge(const, 3)
            pool.wait_ge(rows_in, 48)

            def body(at):
                if tile := at(NORM):
                    j, u = tile
                    t = 2 * j + u
                    pool.wait_ge(gained, t + 1)
                    nc.gpsimd.tensor_tensor(out=h1[:, u, :], in0=h1[:, u, :], in1=shift[:, :],
                                            op=ALU.add).then_inc(h1_ready, 1)
                if tile := at(STATS):
                    j, u = tile
                    t = 2 * j + u
                    pool.wait_ge(var_ready, t + 1)
                    nc.gpsimd.tensor_tensor(out=rstd[:, u, :], in0=var_eps[:, u, :],
                                            in1=minus_half[:, :], op=ALU.pow).then_inc(rstd_ready, 1)

            ticks(pool, TT, DEPTH4, body)

        @block.scalar
        def _(act):
            for dst, name in ((bias, "b_out"), (gain, "ln1_g"), (shift, "ln1_b")):
                act.dma_start(dst[:, :], io[name].partition_broadcast(P)).then_inc(rows_in, 16)
            for k in range(KD):
                act.wait_ge(w_in[k % 2], 16 * (KD // 2))
                nc.scalar.activation(w_hi[:, k, :], w_raw[:, k, :], ACT.Copy).then_inc(whi, 1)

            def body(at):
                if tile := at(TURN):
                    j, u = tile
                    t = 2 * j + u
                    act.wait_ge(transposed, t + 1 + CREDITS)
                    act.wait_ge(h1T_stored[u], 16 + 32 * j)
                    nc.scalar.activation(h1T_hi[:, u, :, :].rearrange("p k t -> p (k t)"), tp[u][:, :],
                                         ACT.Copy).then_inc(hhi_ready, 1)

            ticks(act, TT, DEPTH4, body)

        @block.vector
        def _(dve):
            for k in range(KD):
                dve.wait_ge(whi, k + 1)
                nc.vector.tensor_tensor(out=w_lo[:, k, :], in0=w_raw[:, k, :], in1=f32(w_hi[:, k, :]),
                                        op=ALU.subtract).then_inc(wlo, 1)
            dve.wait_ge(rows_in, 48)

            def body(at):
                if tile := at(NORM):
                    j, u = tile
                    t = 2 * j + u
                    dve.wait_ge(rstd_ready, t + 1)
                    dve.wait_ge(transposed, t + 1)
                    dve.wait_ge(h1_stored[u], 16 * (j + 1))
                    nc.vector.tensor_scalar(h1[:, u, :], res[:, u, :], mean_var[:, u, 0:1],
                                            rstd[:, u, :], ALU.subtract, ALU.mult).then_inc(normed, 1)
                    dve.wait_ge(normed, t + 1 + CREDITS)
                    nc.vector.tensor_tensor(out=h1[:, u, :], in0=h1[:, u, :], in1=gain[:, :],
                                            op=ALU.mult).then_inc(gained, 1)
                if tile := at(STATS):
                    j, u = tile
                    t = 2 * j + u
                    dve.wait_ge(summed, t + 1 + CREDITS)
                    nc.vector.bn_stats(stats[:, u, 0:6], res[:, u, 0:D // 2])
                    nc.vector.bn_stats(stats[:, u, 6:12], res[:, u, D // 2:D]).then_inc(stats_step, 1)
                    whole(dve, top, (stats_step, 2 * t + 1))
                    nc.vector.bn_aggr(mean_var[:, u, :], stats[:, u, :]).then_inc(stats_step, 1)
                    dve.wait_ge(stats_step, 2 * t + 2)
                    nc.vector.tensor_scalar(var_eps[:, u, :], mean_var[:, u, 1:2], EPS, None,
                                            ALU.add).then_inc(var_ready, 1)
                if tile := at(TURN):
                    j, u = tile
                    t = 2 * j + u
                    dve.wait_ge(hhi_ready, t + 1)
                    nc.vector.tensor_tensor(out=h1T_lo[:, u, :, :].rearrange("p k t -> p (k t)"),
                                            in0=tp[u][:, :],
                                            in1=f32(h1T_hi[:, u, :, :]).rearrange("p k t -> p (k t)"),
                                            op=ALU.subtract).then_inc(hlo_ready, 1)
                if tile := at(MIX):
                    j, u = tile
                    t = 2 * j + u
                    dve.wait_ge(h0_in[u], 16 * (j + 1))
                    nc.vector.scalar_tensor_tensor(h0[:, u, :], h0[:, u, :], ALPHA, bias[:, :],
                                                   ALU.mult, ALU.add).then_inc(carried, 1)
                    dve.wait_ge(mixed, t + 1)
                    dve.wait_ge(carried, t + 1)
                    dve.wait_ge(normed, t + 1)
                    nc.vector.tensor_tensor(out=res[:, u, :], in0=h0[:, u, :], in1=mix[u][:, :],
                                            op=ALU.add).then_inc(summed, 1)

            ticks(dve, TT, DEPTH4, body)

        @block.tensor
        def _(pe):
            pe.wait_ge(const, 2)

            def body(at):
                if tile := at(TURN):
                    j, u = tile
                    t = 2 * j + u
                    pe.wait_ge(h1_ready, t + 1)
                    pe.wait_ge(hlo_ready, t + 1)
                    for k in range(KD):
                        last = nc.tensor.transpose(tp[u][:, bass.ts(k, P)], h1[:, u, bass.ts(k, P)],
                                                   ident[:, :])
                    last.then_inc(transposed, 1)
                if tile := at(MIX):
                    j, u = tile
                    t = 2 * j + u
                    first = isinstance(t, int) and t == 0
                    pe.wait_ge(y_in[u], 32 * (j + 1))
                    pe.wait_ge(summed, t + 1)
                    for k in range(KD):
                        if first:
                            pe.wait_ge(wlo, k + 1)
                        last = token_major(nc.tensor, mix[u], y_hi[:, u, k, :], y_lo[:, u, k, :],
                                           w_hi[:, k, :], w_lo[:, k, :], k == 0, k == KD - 1)
                    last.then_inc(mixed, 1)

            ticks(pe, TT, DEPTH4, body)
    m.stack.close()
    return [(h1_stored[u], 16 + 16 * TT // 2) for u in range(2)] + [
        (h1T_stored[u], 16 + 32 * TT // 2) for u in range(2)]


def load_block(sp, scr, hT_hi, hT_lo, hT_in, b):
    for part, dst in ((0, hT_hi), (1, hT_lo)):
        sp.dma_start(f32(dst[b][:, :, :]),
                     scr["h1T"][part, :, :, bass.ts(b, BLK)].rearrange("k p t -> p k t")
                     ).then_inc(hT_in[b], 16)


def load_up_chunk(sp, io, w_raw, w_in, t, c):
    cols = io["ffn_w_up"][:, bass.ds(t * P + c * FF, P)]
    sp.dma_start(w_raw[:, c, :, :], cols.rearrange("(k p) n -> p k n", p=P)).then_inc(w_in[c], 16)


def load_step(sp, io, scr, w_raw, g_raw, raw_in, t, k):
    sp.dma_start(w_raw[:, k % 2, :], io["ffn_w_down"][bass.ts(k, P), :]).then_inc(raw_in[k % 2], 16)
    sp.dma_start(g_raw[:, k % 2, :], scr["hidden"][k, :, bass.ts(t, BLK)]).then_inc(raw_in[k % 2], 16)


def phase5(nc, top, io, scr, first_hi, first_lo, hT_in, w_raw, w_in, spare, stored,
           load_next):
    m = top.phase()
    w_hi = m.sb("w_hi5", [2, KD, P], F32R)
    w_lo = m.sb("w_lo5", [2, KD, P], F32R)
    vecs = m.sb("ffn_vectors", [FW + 2, 2 * NF])
    hT_hi = [first_hi] + [m.sb(f"h1T_hi{b}", [KD, BLK], F32R) for b in range(1, NB)]
    hT_lo = [first_lo] + [m.sb(f"h1T_lo{b}", [KD, BLK], F32R) for b in range(1, NB)]
    spare = spare[:, :, :].rearrange("p k n -> p (k n)")
    UP = FW - 1 + T
    up = [spare[:, 0:UP], spare[:, UP:2 * UP]]
    value = spare[:, 2 * UP:2 * UP + T]
    gate = spare[:, 2 * UP + T:2 * UP + T + 2 * BLK].rearrange("p (s n) -> p s n", s=2)
    TAP, CONV_B, B_UP = 0, FW, FW + 1
    mm = [m.ps(f"mm5_{i}", BLK) for i in range(2)]

    hidden_stored = top.sem("hidden_stored5", 2)
    (consts_in, pad_ready, whi, w_split, mm_ready, evac, conv_step, value_done, gate_done, gelu_done,
     hidden_ready) = (top.sem(n + "_5") for n in (
        "consts_in", "pad_ready", "whi", "w_split", "mm_ready", "evac", "conv_step", "value_done",
        "gate_done", "gelu_done", "hidden_ready"))
    VALUE, GATE = range(2)
    GROUPS = 2 * NB
    MM0 = 2 * NB
    BY_CHUNK = [(c, b) for c in range(2) for b in range(NB)]
    BY_BLOCK = [(c, b) for b in range(NB) for c in range(2)]

    def run(eng, body):
        body(0, BY_BLOCK)
        with eng.Fori(1, NF - 1) as t:
            body(t, BY_CHUNK)
        body(NF - 1, BY_CHUNK)

    def coming(t, order, n):
        if order is BY_BLOCK:
            return (1, VALUE) if n == GROUPS - 1 else None
        if n == 0:
            return t, GATE
        last = isinstance(t, int)
        return (t + 1, VALUE) if n == NB and not last else None

    with nc.Block() as block:
        @block.sync
        def _(sp):
            for s, n in ((w_split, CREDITS), (evac, CREDITS), (mm_ready, MM0), (value_done, 1),
                         (gate_done, 1), (hidden_ready, CREDITS)):
                sp.sem_inc(s, n)
            for u in range(2):
                sp.sem_inc(hidden_stored[u], 16)

            def load(t, c):
                whole(sp, top, (w_split, 2 * t + c + 1))
                load_up_chunk(sp, io, w_raw, w_in, t, c)

            for sem, count in stored:
                sp.wait_ge(sem, count)
            for b in range(1, NB):
                load_block(sp, scr, hT_hi, hT_lo, hT_in, b)

            def body(t, order):
                last = isinstance(t, int) and t > 0
                if last:
                    for u in range(2):
                        sp.wait_ge(hidden_stored[u], 16 + 16 * NB)
                    load_next(sp)
                for c, b in order:
                    if b == 0 and not last:
                        load(t + 1, c)
                    if c == GATE:
                        whole(sp, top, (hidden_ready, NB * t + b + 1 + CREDITS))
                        sp.dma_start(scr["hidden"][bass.ds(t, 1), :, bass.ts(b, BLK)]
                                     .rearrange("k p t -> p (k t)"), gate[:, b % 2, :]
                                     ).then_inc(hidden_stored[b % 2], 16)

            run(sp, body)
        @block.gpsimd
        def _(pool):
            for buf in up:
                nc.gpsimd.memset(buf[:, 0:FW - 1], 0.0).then_inc(pad_ready, 1)

        @block.scalar
        def _(act):
            act.dma_start(vecs[:, :, :], io["ffn_vectors"]).then_inc(consts_in, 16)

            def hi(t, c, products):
                act.wait_ge(w_in[c], 16 * t + 16)
                act.wait_ge(mm_ready, products + MM0)
                nc.scalar.activation(w_hi[:, c, :, :].rearrange("p k n -> p (k n)"),
                                     w_raw[:, c, :, :].rearrange("p k n -> p (k n)"),
                                     ACT.Copy).then_inc(whi, 1)

            hi(0, VALUE, 0)
            hi(0, GATE, 0)
            act.wait_ge(consts_in, 16)

            def body(t, order):
                for n, (c, b) in enumerate(order):
                    whole(act, top, (mm_ready, GROUPS * t + n + 1 + MM0),
                          ((value_done, gate_done)[c], NB * t + 1))
                    nc.scalar.activation(up[c][:, bass.ds(FW - 1 + b * BLK, BLK)], mm[n % 2][:, :],
                                         ACT.Identity, bias=vecs[:, B_UP, bass.ds(t + c * NF, 1)]
                                         ).then_inc(evac, 1)
                    if chunk := coming(t, order, n):
                        done = GROUPS * t + (n if c == GATE else 0)
                        hi(*chunk, done)
                    if c == GATE:
                        act.wait_ge(gate_done, NB * t + b + 2)
                        nc.scalar.activation(gate[:, b % 2, :], gate[:, b % 2, :],
                                             ACT.Gelu_apprx_tanh).then_inc(gelu_done, 1)

            run(act, body)

        @block.vector
        def _(dve):
            def lo(t, c):
                dve.wait_ge(whi, 2 * t + c + 1)
                nc.vector.tensor_tensor(out=w_lo[:, c, :, :].rearrange("p k n -> p (k n)"),
                                        in0=w_raw[:, c, :, :].rearrange("p k n -> p (k n)"),
                                        in1=f32(w_hi[:, c, :, :]).rearrange("p k n -> p (k n)"),
                                        op=ALU.subtract).then_inc(w_split, 1)

            lo(0, VALUE)
            lo(0, GATE)
            dve.wait_ge(pad_ready, 2)

            def body(t, order):
                for n, (c, b) in enumerate(order):
                    vec = lambda row: vecs[:, row, bass.ds(t + c * NF, 1)]
                    dve.wait_ge(evac, GROUPS * t + n + 1 + CREDITS)
                    if c == VALUE:
                        dve.wait_ge(hidden_ready, NB * t + CREDITS)
                        out, done = value[:, bass.ts(b, BLK)], value_done
                    else:
                        dve.wait_ge(hidden_stored[b % 2], 16 + 16 * (2 * t + b // 2))
                        out, done = gate[:, b % 2, :], gate_done
                    nc.vector.tensor_scalar(out, up[c][:, bass.ds(b * BLK, BLK)], vec(TAP),
                                            vec(CONV_B), ALU.mult, ALU.add).then_inc(conv_step, 1)
                    for k in range(1, FW):
                        dve.wait_ge(conv_step, (FW - 1) * (GROUPS * t + n) + k)
                        nc.vector.scalar_tensor_tensor(
                            out, up[c][:, bass.ds(b * BLK + k, BLK)], vec(TAP + k), out,
                            ALU.mult, ALU.add).then_inc(conv_step if k < FW - 1 else done, 1)
                    if chunk := coming(t, order, n):
                        lo(*chunk)
                    if c == GATE:
                        dve.wait_ge(gelu_done, NB * t + b + 1)
                        nc.vector.tensor_tensor(out=gate[:, b % 2, :], in0=gate[:, b % 2, :],
                                                in1=value[:, bass.ts(b, BLK)], op=ALU.mult
                                                ).then_inc(hidden_ready, 1)

            run(dve, body)

        @block.tensor
        def _(pe):
            def body(t, order):
                for n, (c, b) in enumerate(order):
                    if b == 0:
                        pe.wait_ge(w_split, 2 * t + c + 1 + CREDITS)
                    if c == VALUE:
                        pe.wait_ge(hT_in[b], 32)
                    pe.wait_ge(evac, GROUPS * t + n + 1)
                    for k in range(KD):
                        done = three_passes(nc.tensor, mm[n % 2][:, :], w_hi[:, c, k, :],
                                            w_lo[:, c, k, :], hT_hi[b][:, k, :],
                                            hT_lo[b][:, k, :], k == 0, k == KD - 1)
                    done.then_inc(mm_ready, 1)

            run(pe, body)
    m.stack.close()
    return [(hidden_stored[u], 16 + 16 * NB * NF // 2) for u in range(2)]


def phase6(nc, top, io, scr, out, w_raw, g_raw, raw_in, stored):
    m = top.phase()
    w_hi = m.sb("wd_hi", [2, D], F32R)
    w_lo = m.sb("wd_lo", [2, D], F32R)
    g_hi = m.sb("hidden_hi", [2, BLK], F32R)
    g_lo = m.sb("hidden_lo", [2, BLK], F32R)
    h1 = m.sb("h1_block", [TPB, D])
    res = m.sb("residual6", [TPB, D])
    y = m.sb("out_block", [TPB, D])
    bias = m.sb("b_down_row", [D])
    gain = m.sb("ln2_gain", [D])
    shift = m.sb("ln2_shift", [D])
    stats = m.sb("stats6", [TPB, 12])
    mean_var = m.sb("mean_var6", [TPB, 2])
    var_eps = m.sb("var_eps6", [TPB, 1])
    minus_half = m.sb("minus_half6", [1])
    rstd = m.sb("rstd6", [TPB, 1])
    acc = [m.ps(f"down{i}", D) for i in range(TPB)]

    out_stored = top.sem("out_stored6", TPB)
    (rows_in, const, h1_in, hi_ready, split, used, tile_done, summed, carried, stats_step,
     var_ready, rstd_ready, normed, gained, out_ready) = (top.sem(n + "_6") for n in (
        "rows_in", "const", "h1_in", "hi_ready", "split", "used", "tile_done", "summed", "carried",
        "stats_step", "var_ready", "rstd_ready", "normed", "gained", "out_ready"))
    HEAD = 12

    STATS_AT, NORM_AT = ({2 * i + d: i for i in range(TPB)} for d in range(1, 3))
    CARRY_AT = {HEAD + 2 + i: i for i in range(TPB)}

    def run(engine_round, step, beside, evacuate):
        for k in range(HEAD):
            step(0, k)

        def body(t):
            last = isinstance(t, int)
            for k in range(HEAD, NF):
                step(t, k)
            evacuate(t)
            for k in range(HEAD):
                if not last:
                    step(t + 1, k)
                beside(t, k)

        rounds(engine_round, NB, body)

    with nc.Block() as block:
        @block.sync
        def _(sp):
            for s, n in ((split, CREDITS), (used, CREDITS), (summed, TPB), (normed, TPB)):
                sp.sem_inc(s, n)
            for i in range(TPB):
                sp.sem_inc(out_stored[i], 16)

            def load(t, k):
                whole(sp, top, (split, NF * t + k + 1))
                load_step(sp, io, scr, w_raw, g_raw, raw_in, t, k)

            def load_residual(t):
                whole(sp, top, (summed, TPB * t + TPB))
                sp.dma_start(h1[:, :, :], scr["h1"][bass.ts(t, BLK), :]
                             .rearrange("(i p) d -> p i d", p=P)).then_inc(h1_in, 16)

            def step(t, k):
                if isinstance(t, int) and t == 0 and k < 2:
                    return
                if isinstance(t, int) and t == 0 and k == 2:
                    for sem, count in stored:
                        sp.wait_ge(sem, count)
                load(t, k)
                if k == HEAD:
                    load_residual(t)

            def beside(t, k):
                if k >= 5 and k % 2 == 1:
                    i = (k - 5) // 2
                    whole(sp, top, (out_ready, TPB * t + i + 1))
                    sp.dma_start(out[bass.ds(t * BLK + i * P, P), :], y[:, i, :]
                                 ).then_inc(out_stored[i], 16)

            run(sp, step, beside, lambda t: None)
            for i in range(TPB):
                sp.wait_ge(out_stored[i], 16 + 16 * NB)

        @block.gpsimd
        def _(pool):
            nc.gpsimd.memset(minus_half[:, :], -0.5).then_inc(const, 1)
            pool.wait_ge(const, 1)
            pool.wait_ge(rows_in, 48)

            def power(t, i):
                pool.wait_ge(var_ready, TPB * t + i + 1)
                nc.gpsimd.tensor_tensor(out=rstd[:, i, :], in0=var_eps[:, i, :],
                                        in1=minus_half[:, :], op=ALU.pow).then_inc(rstd_ready, 1)

            def add_shift(t, i):
                pool.wait_ge(gained, TPB * t + i + 1)
                nc.gpsimd.tensor_tensor(out=y[:, i, :], in0=y[:, i, :], in1=shift[:, :],
                                        op=ALU.add).then_inc(out_ready, 1)

            def beside(t, k):
                if k in STATS_AT:
                    power(t, STATS_AT[k])
                if k in NORM_AT:
                    add_shift(t, NORM_AT[k])

            run(pool, lambda t, k: None, beside, lambda t: None)

        @block.scalar
        def _(act):
            for dst, name in ((bias, "ffn_b_down"), (gain, "ln2_g"), (shift, "ln2_b")):
                act.dma_start(dst[:, :], io[name].partition_broadcast(P)).then_inc(rows_in, 16)

            def step(t, k):
                act.wait_ge(raw_in[k % 2], 32 * (NF // 2 * t + k // 2 + 1))
                act.wait_ge(used, NF * t + k + 1)
                nc.scalar.activation(w_hi[:, k % 2, :], w_raw[:, k % 2, :], ACT.Copy)
                nc.scalar.activation(g_hi[:, k % 2, :], g_raw[:, k % 2, :], ACT.Copy
                                     ).then_inc(hi_ready, 1)

            run(act, step, lambda t, k: None, lambda t: None)

        @block.vector
        def _(dve):
            dve.wait_ge(rows_in, 48)

            def step(t, k):
                dve.wait_ge(hi_ready, NF * t + k + 1)
                nc.vector.tensor_tensor(out=w_lo[:, k % 2, :], in0=w_raw[:, k % 2, :],
                                        in1=f32(w_hi[:, k % 2, :]), op=ALU.subtract)
                nc.vector.tensor_tensor(out=g_lo[:, k % 2, :], in0=g_raw[:, k % 2, :],
                                        in1=f32(g_hi[:, k % 2, :]), op=ALU.subtract
                                        ).then_inc(split, 1)
                if k in CARRY_AT:
                    i = CARRY_AT[k]
                    if i == 0:
                        dve.wait_ge(h1_in, 16 * t + 16)
                    nc.vector.scalar_tensor_tensor(h1[:, i, :], h1[:, i, :], ALPHA, bias[:, :],
                                                   ALU.mult, ALU.add).then_inc(carried, 1)

            def evacuate(t):
                for i in range(TPB):
                    if i == 0:
                        dve.wait_ge(carried, TPB * t + TPB)
                        dve.wait_ge(normed, TPB * t + TPB)
                    if i < TPB - 1:
                        dve.wait_ge(tile_done, (TPB - 1) * t + i + 1)
                    else:
                        dve.wait_ge(used, NF * t + NF + CREDITS)
                    nc.vector.tensor_tensor(out=res[:, i, :], in0=h1[:, i, :], in1=acc[i][:, :],
                                            op=ALU.add).then_inc(summed, 1)

            def beside(t, k):
                if k in STATS_AT:
                    i = STATS_AT[k]
                    n = TPB * t + i
                    dve.wait_ge(summed, n + 1 + TPB)
                    nc.vector.bn_stats(stats[:, i, 0:6], res[:, i, 0:D // 2])
                    nc.vector.bn_stats(stats[:, i, 6:12], res[:, i, D // 2:D]).then_inc(stats_step, 1)
                    whole(dve, top, (stats_step, 2 * n + 1))
                    nc.vector.bn_aggr(mean_var[:, i, :], stats[:, i, :]).then_inc(stats_step, 1)
                    dve.wait_ge(stats_step, 2 * n + 2)
                    nc.vector.tensor_scalar(var_eps[:, i, :], mean_var[:, i, 1:2], EPS, None,
                                            ALU.add).then_inc(var_ready, 1)
                if k in NORM_AT:
                    i = NORM_AT[k]
                    n = TPB * t + i
                    dve.wait_ge(rstd_ready, n + 1)
                    dve.wait_ge(out_stored[i], 16 * t + 16)
                    nc.vector.tensor_scalar(y[:, i, :], res[:, i, :], mean_var[:, i, 0:1],
                                            rstd[:, i, :], ALU.subtract, ALU.mult).then_inc(normed, 1)
                    dve.wait_ge(normed, n + 1 + TPB)
                    nc.vector.tensor_tensor(out=y[:, i, :], in0=y[:, i, :], in1=gain[:, :],
                                            op=ALU.mult).then_inc(gained, 1)

            run(dve, step, beside, evacuate)

        @block.tensor
        def _(pe):
            def step(t, k):
                pe.wait_ge(split, NF * t + k + 1 + CREDITS)
                for i in range(TPB):
                    if k == 0:
                        pe.wait_ge(summed, TPB * t + i + 1)
                    done = token_major(nc.tensor, acc[i], g_hi[:, k % 2, bass.ts(i, P)],
                                       g_lo[:, k % 2, bass.ts(i, P)], w_hi[:, k % 2, :],
                                       w_lo[:, k % 2, :], k == 0, k == NF - 1)
                    if i == TPB - 1:
                        done.then_inc(used, 1)
                    elif k == NF - 1:
                        done.then_inc(tile_done, 1)

            run(pe, step, lambda t, k: None, lambda t: None)
    m.stack.close()


def program(nc, io, out, scratch, phases=(1, 2, 3, 4, 5, 6)):
    scr = {name: scratch(name, shape) for name, shape in (
        ("h0", [T, D]), ("v", [2, T, DA]), ("q", [2, NA, P, T]),
        ("k", [2, NA, P, T]), ("yT", [2, KD, P, T]), ("h1", [T, D]), ("h1T", [2, KD, P, T]),
        ("hidden", [NF, P, T]), ("bias_ext", [HEADS, BIAS_EXT]),
        ("bias_rows", [P, HEADS, BIAS_EXT]))}
    with ExitStack() as stack:
        top = Tools(nc, stack)
        top.started = top.sem("started")
        with nc.Block() as block:
            @block.sync
            def _(sp):
                sp.sem_inc(top.started, 1)

        held = top.phase()
        hT_hi, hT_lo = (held.sb(n, [KD, T], F32R) for n in ("hT_hi", "hT_lo"))
        w_raw, w_in = held.sb("w_raw", [2, KD, P]), top.sem("w_in_loaded", 2)

        def load_first_chunks(sp):
            for c in range(2):
                load_chunk(sp, io, w_raw, w_in, 0, c)

        if 1 in phases:
            phase1(nc, top, io, scr, hT_hi, hT_lo, w_raw, load_first_chunks)
        stored = []
        if 2 in phases:
            stored = phase2(nc, top, io, scr, hT_hi, hT_lo, w_raw, w_in)
        held.stack.close()
        rows = top.phase()
        out_raw, out_in = rows.sb("out_raw", [KD, D]), top.sem("out_in", 2)

        def load_for_4(sp):
            for k in range(KD):
                sp.dma_start(out_raw[:, k, :], io["w_out"][bass.ts(k, P), :]).then_inc(out_in[k % 2], 16)

        if 3 in phases:
            phase3(nc, top, io, scr, stored, load_for_4)
        held = top.phase()
        first_hi, first_lo = (held.sb(n, [KD, BLK], F32R) for n in ("h1T_hi0", "h1T_lo0"))
        up_raw, up_in, h1T_in = held.sb("up_raw", [2, KD, P]), top.sem("up_in", 2), top.sem("h1T_in", NB)

        def load_for_5(sp):
            load_block(sp, scr, [first_hi], [first_lo], h1T_in, 0)
            for c in range(2):
                load_up_chunk(sp, io, up_raw, up_in, 0, c)

        if 4 in phases:
            stored = phase4(nc, top, io, scr, out_raw, out_in, load_for_5)
        late = top.phase()
        down_raw, hidden_raw = late.sb("down_raw", [2, D]), late.sb("hidden_raw", [2, BLK])
        raw_in = top.sem("down_raw_in", 2)

        def load_for_6(sp):
            for k in range(2):
                load_step(sp, io, scr, down_raw, hidden_raw, raw_in, 0, k)

        if 5 in phases:
            stored = phase5(nc, top, io, scr, first_hi, first_lo, h1T_in, up_raw, up_in, out_raw,
                            stored, load_for_6)
        if 6 in phases:
            phase6(nc, top, io, scr, out, down_raw, hidden_raw, raw_in, stored)
        late.stack.close()
        held.stack.close()
        rows.stack.close()


def host_layout(inputs):
    a = {k: np.ascontiguousarray(v) for k, v in inputs.items()}
    out = {n: a[n].reshape(a[n].shape[1:]) for n in a if n not in ("ln_in_g", "ln_in_b")}
    out["ln_in_g"], out["ln_in_b"] = a["ln_in_g"], a["ln_in_b"]
    by_tile = lambda v: np.ascontiguousarray(v.reshape(-1, P).T)
    lru = [a["lru_conv_w"][0, k] for k in range(CW)]
    lru += [a[n][0] for n in ("lru_conv_b", "lru_b_a", "lru_b_x", "lru_lambda")]
    out["lru_vectors"] = np.ascontiguousarray(np.stack([by_tile(v) for v in lru], axis=1))
    out["b_in"] = by_tile(a["b_in"][0])
    ffn = [a["ffn_conv_w"][0, k] for k in range(FW)] + [a["ffn_conv_b"][0], a["ffn_b_up"][0]]
    out["ffn_vectors"] = np.ascontiguousarray(np.stack([by_tile(v) for v in ffn], axis=1))
    gate_w = np.zeros((NA, P, 2, P), np.float32)
    for g, name in enumerate(("lru_w_a", "lru_w_x")):
        for n, w in enumerate(a[name][0]):
            s = slice(HD * (n % 2), HD * (n % 2) + HD)
            gate_w[n // 2, s, g, s] = w
    out["gate_w"] = gate_w
    out["rel_bias_reversed"] = np.ascontiguousarray(a["rel_bias"][0, :, ::-1])
    out["bias_far"] = np.ascontiguousarray(a["rel_bias"][0, :, -1])
    for n in ("rel_bias", "lru_conv_w", "lru_conv_b", "lru_b_a", "lru_b_x", "lru_lambda", "lru_w_a",
              "lru_w_x", "ffn_conv_w", "ffn_conv_b", "ffn_b_up"):
        del out[n]
    return out


def kernel(**inputs):
    import concourse.bacc as bacc
    from concourse.bass_utils import run_bass_kernel_spmd as run

    nc = bacc.Bacc("TRN2", target_bir_lowering=False, num_devices=1)
    arrays = {f"in_{name}": a for name, a in host_layout(inputs).items()}
    io = {name[3:]: nc.dram_tensor(name, a.shape, F32, kind="ExternalInput").ap()
          for name, a in arrays.items()}
    out = nc.dram_tensor("out", [T, D], F32, kind="ExternalOutput").ap()

    def scratch(name, shape):
        return nc.dram_tensor(f"scratch_{name}", shape, F32, kind="Internal").ap()

    program(nc, io, out, scratch)
    result = run(nc, [arrays], core_ids=[0])
    return result.results[0]["out"].reshape(inputs["x"].shape)
```
